# Optimizing a Trainium2 kernel written in Bass

```python
import jax, jax.numpy as jnp
from jax import lax
import numpy as np
import math
import jax
import jax.numpy as jnp

D_MODEL = 1024
BATCH = 1
SEQ = 512
DEPTH = 1

CONV_WIDTH = 512
CONV_KERNEL = 31
N_HEADS = 8
QK_NOPE_DIM = 64
QK_ROPE_DIM = 32
V_HEAD_DIM = 64
Q_LORA_RANK = 384
KV_LORA_RANK = 256
ROPE_THETA = 10000.0
Q_BLOCK = 128
QK_HEAD_DIM = QK_NOPE_DIM + QK_ROPE_DIM
MLA_WIDTH = N_HEADS * V_HEAD_DIM
D_FF = 2816
FFN_KERNEL = 3
N_BRANCHES = 2
NORM_EPS = 1e-6
IN_SPLITS = (2 * CONV_WIDTH, Q_LORA_RANK, KV_LORA_RANK, QK_ROPE_DIM, N_BRANCHES * D_MODEL)
D_IN = 2 * CONV_WIDTH + Q_LORA_RANK + KV_LORA_RANK + QK_ROPE_DIM + N_BRANCHES * D_MODEL


def rms_norm(x, g):
    xf = x.astype(jnp.float32)
    y = xf * lax.rsqrt(jnp.mean(xf * xf, axis=-1, keepdims=True) + NORM_EPS)
    return (y * g.astype(jnp.float32)).astype(x.dtype)

def layer_norm(x, g, b):
    xf = x.astype(jnp.float32)
    mu = jnp.mean(xf, axis=-1, keepdims=True)
    xc = xf - mu
    y = xc * lax.rsqrt(jnp.mean(xc * xc, axis=-1, keepdims=True) + NORM_EPS)
    return (y * g.astype(jnp.float32) + b.astype(jnp.float32)).astype(x.dtype)

def depthwise_conv(x, w, b):
    k, c = w.shape
    pad = k // 2
    y = lax.conv_general_dilated(
        x, w[:, None, :].astype(x.dtype), window_strides=(1,), padding=[(pad, pad)],
        dimension_numbers=("NWC", "WIO", "NWC"), feature_group_count=c)
    return y + b

def split_cols(t, sizes):
    out, off = [], 0
    for s in sizes:
        out.append(t[..., off:off + s])
        off += s
    return out

def rope_tables(positions):
    inv_freq = 1.0 / (ROPE_THETA ** (jnp.arange(0, QK_ROPE_DIM, 2, dtype=jnp.float32) / QK_ROPE_DIM))
    ang = positions.astype(jnp.float32)[..., None] * inv_freq
    return jnp.cos(ang), jnp.sin(ang)

def apply_rope(t, cos, sin):
    tf = t.astype(jnp.float32)
    t1, t2 = tf[..., : QK_ROPE_DIM // 2], tf[..., QK_ROPE_DIM // 2:]
    return jnp.concatenate([t1 * cos - t2 * sin, t2 * cos + t1 * sin], axis=-1).astype(t.dtype)

def conformer_conv(a, dw_w, dw_b, ln_g, ln_b, w_out, b_out):
    val, gate = a[..., :CONV_WIDTH], a[..., CONV_WIDTH:]
    u = val * jax.nn.sigmoid(gate)
    u = depthwise_conv(u, dw_w, dw_b)
    u = jax.nn.silu(layer_norm(u, ln_g, ln_b))
    return u @ w_out + b_out

def mla(q_c, kv_c, k_rope_in, positions, q_norm_g, w_uq, kv_norm_g, w_ukv, w_mla_out):
    b, s, _ = q_c.shape
    q = (rms_norm(q_c, q_norm_g) @ w_uq).reshape(b, s, N_HEADS, QK_HEAD_DIM)
    q_nope, q_rope = q[..., :QK_NOPE_DIM], q[..., QK_NOPE_DIM:]
    kv = (rms_norm(kv_c, kv_norm_g) @ w_ukv).reshape(b, s, N_HEADS, QK_NOPE_DIM + V_HEAD_DIM)
    k_nope, v = kv[..., :QK_NOPE_DIM], kv[..., QK_NOPE_DIM:]
    cos, sin = rope_tables(positions)
    q_rope = apply_rope(q_rope, cos[:, :, None, :], sin[:, :, None, :])
    k_rope = apply_rope(k_rope_in, cos, sin)
    scale = QK_HEAD_DIM ** -0.5
    n_blk = s // Q_BLOCK

    def to_blocks(t):
        return jnp.moveaxis(t.reshape(b, n_blk, Q_BLOCK, *t.shape[2:]), 1, 0)

    def attend(blk):
        qn, qr = blk
        sc = (jnp.einsum('bqhd,bkhd->bhqk', qn, k_nope)
              + jnp.einsum('bqhr,bkr->bhqk', qr, k_rope)).astype(jnp.float32) * scale
        p = jax.nn.softmax(sc, axis=-1).astype(v.dtype)
        return jnp.einsum('bhqk,bkhd->bqhd', p, v)

    o = lax.map(attend, (to_blocks(q_nope), to_blocks(q_rope)))
    o = jnp.moveaxis(o, 0, 1).reshape(b, s, MLA_WIDTH)
    return o @ w_mla_out

def conv_ffn(h, w_up, dw_w, dw_b, w_down):
    gu = depthwise_conv(h @ w_up, dw_w, dw_b)
    gate, up = gu[..., :D_FF], gu[..., D_FF:]
    return (jax.nn.silu(gate) * up) @ w_down

def first_inputs(seed: int = 0) -> dict:
    key = jax.random.key(seed)
    ks = iter(jax.random.split(key, 32))

    def w(shape, fan_in):
        return jax.random.normal(next(ks), shape, jnp.float32) * (fan_in ** -0.5)

    def gain(shape):
        return 1.0 + 0.02 * jax.random.normal(next(ks), shape, jnp.float32)

    def bias(shape):
        return 0.02 * jax.random.normal(next(ks), shape, jnp.float32)

    L = DEPTH
    x = jax.random.normal(next(ks), (BATCH, SEQ, D_MODEL), jnp.float32)
    offset = jax.random.randint(next(ks), (BATCH, 1), 0, SEQ, dtype=jnp.int32)
    positions = offset + jnp.arange(SEQ, dtype=jnp.int32)[None, :]
    return {
        "x": x,
        "positions": positions,
        "norm1_g": gain((L, D_MODEL)),
        "w_in": w((L, D_MODEL, D_IN), D_MODEL),
        "conv_dw_w": w((L, CONV_KERNEL, CONV_WIDTH), CONV_KERNEL),
        "conv_dw_b": bias((L, CONV_WIDTH)),
        "conv_ln_g": gain((L, CONV_WIDTH)),
        "conv_ln_b": bias((L, CONV_WIDTH)),
        "w_conv_out": w((L, CONV_WIDTH, D_MODEL), CONV_WIDTH),
        "b_conv_out": bias((L, D_MODEL)),
        "q_norm_g": gain((L, Q_LORA_RANK)),
        "w_uq": w((L, Q_LORA_RANK, N_HEADS * QK_HEAD_DIM), Q_LORA_RANK),
        "kv_norm_g": gain((L, KV_LORA_RANK)),
        "w_ukv": w((L, KV_LORA_RANK, N_HEADS * (QK_NOPE_DIM + V_HEAD_DIM)), KV_LORA_RANK),
        "w_mla_out": w((L, MLA_WIDTH, D_MODEL), MLA_WIDTH),
        "w_out": w((L, D_MODEL, D_MODEL), D_MODEL),
        "norm2_g": gain((L, D_MODEL)),
        "w_ffn_up": w((L, D_MODEL, 2 * D_FF), D_MODEL),
        "ffn_dw_w": w((L, FFN_KERNEL, 2 * D_FF), FFN_KERNEL),
        "ffn_dw_b": bias((L, 2 * D_FF)),
        "w_ffn_down": w((L, D_FF, D_MODEL), D_FF),
        "norm_f_g": gain((D_MODEL,)),
    }

def first_block(x, positions, norm1_g, w_in, conv_dw_w, conv_dw_b, conv_ln_g, conv_ln_b,
              w_conv_out, b_conv_out, q_norm_g, w_uq, kv_norm_g, w_ukv, w_mla_out, w_out,
              norm2_g, w_ffn_up, ffn_dw_w, ffn_dw_b, w_ffn_down, norm_f_g):
    for l in range(DEPTH):
        h = rms_norm(x, norm1_g[l])
        proj = h @ w_in[l]
        a_in, q_c, kv_c, k_rope_in, gates = split_cols(proj, IN_SPLITS)
        y_conv = conformer_conv(a_in, conv_dw_w[l], conv_dw_b[l], conv_ln_g[l], conv_ln_b[l],
                                w_conv_out[l], b_conv_out[l])
        y_mla = mla(q_c, kv_c, k_rope_in, positions, q_norm_g[l], w_uq[l],
                    kv_norm_g[l], w_ukv[l], w_mla_out[l])
        g = jax.nn.sigmoid(gates.astype(jnp.float32)).astype(x.dtype)
        merged = g[..., :D_MODEL] * y_conv + g[..., D_MODEL:] * y_mla
        x = x + merged @ w_out[l]
        h2 = rms_norm(x, norm2_g[l])
        x = x + conv_ffn(h2, w_ffn_up[l], ffn_dw_w[l], ffn_dw_b[l], w_ffn_down[l])
    return rms_norm(x, norm_f_g)


ATT_HEADS = 8
ATT_HEAD_DIM = 128
KV_LATENT = 256
IDX_HEADS = 8
IDX_DIM = 64
TOPK_MAX = 256
ATT_SCALE = ATT_HEAD_DIM ** -0.5
INDEX_SCALE = (IDX_HEADS ** -0.5) * (IDX_DIM ** -0.5)
DN_HEADS = 8
DN_DK = 128
DN_DV = 128
CONV_WIDTH_2 = 4
CHUNK = 64
N_GROUPS = 4
EXPERTS_PER_GROUP = 8
N_EXPERTS = N_GROUPS * EXPERTS_PER_GROUP
EXPERT_TOPK = 2
EXPERT_FF = 512
MOE_BLOCK = 128
LN_EPS = 1e-5
RMS_EPS = 1e-6

ATT_Q_COLS = ATT_HEADS * ATT_HEAD_DIM
IDX_Q_COLS = IDX_HEADS * IDX_DIM
DN_QK_COLS = DN_HEADS * DN_DK
DN_V_COLS = DN_HEADS * DN_DV
CONV_CH = 2 * DN_QK_COLS + DN_V_COLS
COL_SIZES = (ATT_Q_COLS, KV_LATENT, IDX_Q_COLS, IDX_DIM, IDX_HEADS,
             CONV_CH, DN_HEADS, DN_HEADS, DN_V_COLS, 2 * D_MODEL)
N_IN = sum(COL_SIZES)
SPLITS = tuple(int(v) for v in np.cumsum(COL_SIZES)[:-1])


def layer_norm_2(x, g, b):
    xf = x.astype(jnp.float32)
    mu = jnp.mean(xf, axis=-1, keepdims=True)
    var = jnp.mean(jnp.square(xf - mu), axis=-1, keepdims=True)
    return ((xf - mu) * lax.rsqrt(var + LN_EPS)).astype(x.dtype) * g + b

def rms_norm_2(x, g):
    xf = x.astype(jnp.float32)
    return (xf * lax.rsqrt(jnp.mean(xf * xf, axis=-1, keepdims=True) + RMS_EPS)).astype(x.dtype) * g

def l2_normalize(x):
    return x * lax.rsqrt(jnp.sum(x * x, axis=-1, keepdims=True) + RMS_EPS)

def causal_conv(x, w):
    width = w.shape[0]
    return lax.conv_general_dilated(
        x, w[:, None, :], window_strides=(1,), padding=[(width - 1, 0)],
        dimension_numbers=('NWC', 'WIO', 'NWC'), feature_group_count=x.shape[-1])

def dsa_attention(q_att, c_kv, q_idx, k_idx, w_idx, w_uk, w_uv):
    B, S = c_kv.shape[0], c_kv.shape[1]
    topk = min(TOPK_MAX, S // 4)
    nb = S // Q_BLOCK
    q_lat = jnp.einsum('bshd,hcd->bshc', q_att, w_uk)
    key_pos = jnp.arange(S)
    gather = jax.vmap(lambda table, idx: table[idx])

    def to_blocks(t):
        return jnp.moveaxis(t.reshape((B, nb, Q_BLOCK) + t.shape[2:]), 1, 0)

    def block(args):
        ql, qi, wi, t0 = args
        qpos = t0 + jnp.arange(Q_BLOCK)
        rel = jax.nn.relu(jnp.einsum('bqhd,bsd->bqhs', qi, k_idx))
        iscore = jnp.einsum('bqhs,bqh->bqs', rel, wi).astype(jnp.float32)
        causal = key_pos[None, :] <= qpos[:, None]
        iscore = jnp.where(causal[None], iscore, -jnp.inf)
        _, sel = lax.top_k(iscore, topk)
        kv = gather(c_kv, sel)
        s = jnp.einsum('bqhc,bqkc->bqhk', ql, kv).astype(jnp.float32) * ATT_SCALE
        valid = sel <= qpos[None, :, None]
        s = jnp.where(valid[:, :, None, :], s, -jnp.inf)
        p = jax.nn.softmax(s, axis=-1).astype(kv.dtype)
        return jnp.einsum('bqhk,bqkc->bqhc', p, kv)

    o_lat = lax.map(block, (to_blocks(q_lat), to_blocks(q_idx), to_blocks(w_idx),
                            jnp.arange(nb) * Q_BLOCK))
    o_lat = jnp.moveaxis(o_lat, 0, 1).reshape(B, S, ATT_HEADS, KV_LATENT)
    o = jnp.einsum('bshc,hcd->bshd', o_lat, w_uv)
    return o.reshape(B, S, ATT_HEADS * ATT_HEAD_DIM)

def chunk_gated_delta_rule(q, k, v, beta, g):
    B, S, H, Dk = q.shape
    Dv = v.shape[-1]
    n = S // CHUNK

    def chunks(t):
        return t.reshape(B, n, CHUNK, H, -1).transpose(0, 3, 1, 2, 4)

    q, k, v = chunks(q), chunks(k), chunks(v)
    beta = beta.reshape(B, n, CHUNK, H).transpose(0, 3, 1, 2)
    G = jnp.cumsum(g.reshape(B, n, CHUNK, H).transpose(0, 3, 1, 2), axis=-1)
    tril = jnp.tril(jnp.ones((CHUNK, CHUNK), dtype=bool))
    tril_strict = jnp.tril(jnp.ones((CHUNK, CHUNK), dtype=bool), -1)
    decay = jnp.exp(jnp.where(tril, G[..., :, None] - G[..., None, :], -jnp.inf))
    kb = k * beta[..., None]
    A = jnp.where(tril_strict, jnp.einsum('bhncd,bhnsd->bhncs', kb, k) * decay, 0.0)
    eye = jnp.eye(CHUNK, dtype=A.dtype)
    rhs = jnp.concatenate([v * beta[..., None], kb * jnp.exp(G)[..., None]], axis=-1)
    sol = lax.linalg.triangular_solve(eye + A, rhs, left_side=True, lower=True,
                                      unit_diagonal=True)
    u, w = sol[..., :Dv], sol[..., Dv:]
    qk = jnp.where(tril, jnp.einsum('bhncd,bhnsd->bhncs', q, k) * decay, 0.0)
    q_dec = q * jnp.exp(G)[..., None]
    k_tail = k * jnp.exp(G[..., -1:] - G)[..., None]
    g_last = jnp.exp(G[..., -1])

    def step(state, xs):
        q_n, k_n, u_n, w_n, qk_n, gl_n = xs
        v_new = u_n - jnp.einsum('bhck,bhkv->bhcv', w_n, state)
        o_n = (jnp.einsum('bhck,bhkv->bhcv', q_n, state)
               + jnp.einsum('bhcs,bhsv->bhcv', qk_n, v_new))
        state = state * gl_n[..., None, None] + jnp.einsum('bhck,bhcv->bhkv', k_n, v_new)
        return state, o_n

    xs = tuple(jnp.moveaxis(t, 2, 0) for t in (q_dec, k_tail, u, w, qk, g_last))
    state0 = jnp.zeros((B, H, Dk, Dv), jnp.float32)
    _, o = lax.scan(step, state0, xs)
    return o.transpose(1, 0, 3, 2, 4).reshape(B, S, H, Dv)

def gated_deltanet(qkv, a, b, z, conv_w, a_log, dt_bias, norm_g):
    B, S = qkv.shape[0], qkv.shape[1]
    dtype = qkv.dtype
    qkv = jax.nn.silu(causal_conv(qkv, conv_w)).astype(jnp.float32)
    q = l2_normalize(qkv[..., :DN_QK_COLS].reshape(B, S, DN_HEADS, DN_DK)) * (DN_DK ** -0.5)
    k = l2_normalize(qkv[..., DN_QK_COLS:2 * DN_QK_COLS].reshape(B, S, DN_HEADS, DN_DK))
    v = qkv[..., 2 * DN_QK_COLS:].reshape(B, S, DN_HEADS, DN_DV)
    beta = jax.nn.sigmoid(b.astype(jnp.float32))
    g = -jnp.exp(a_log.astype(jnp.float32)) * jax.nn.softplus(
        a.astype(jnp.float32) + dt_bias.astype(jnp.float32))
    o = chunk_gated_delta_rule(q, k, v, beta, g)
    zf = z.astype(jnp.float32).reshape(B, S, DN_HEADS, DN_DV)
    o = rms_norm_2(o, norm_g.astype(jnp.float32)) * jax.nn.silu(zf)
    return o.reshape(B, S, DN_V_COLS).astype(dtype)

def token_mixer(h, w_in, kv_norm_g, w_uk, w_uv, conv_w, a_log, dt_bias, dn_norm_g,
                w_br_att, w_br_dn, w_out):
    B, S = h.shape[0], h.shape[1]
    proj = h @ w_in
    (q_att, c_kv, q_idx, k_idx, w_idx, qkv, a, b, z, gates) = jnp.split(proj, SPLITS, axis=-1)
    c_kv = rms_norm_2(c_kv, kv_norm_g)
    y_att = dsa_attention(q_att.reshape(B, S, ATT_HEADS, ATT_HEAD_DIM), c_kv,
                          q_idx.reshape(B, S, IDX_HEADS, IDX_DIM), k_idx,
                          w_idx * INDEX_SCALE, w_uk, w_uv)
    y_dn = gated_deltanet(qkv, a, b, z, conv_w, a_log, dt_bias, dn_norm_g)
    gates = jax.nn.sigmoid(gates)
    g_att, g_dn = gates[..., :D_MODEL], gates[..., D_MODEL:]
    merged = g_att * (y_att @ w_br_att) + g_dn * (y_dn @ w_br_dn)
    return merged @ w_out

def hier_moe(h, w_route_grp, w_route_exp, w_gate, w_up, w_down):
    B, S, D = h.shape
    n_tok = B * S
    xt = h.reshape(n_tok, D)
    p_grp = jax.nn.softmax((xt @ w_route_grp).astype(jnp.float32), axis=-1)
    top_gp, g_idx = lax.top_k(p_grp, 1)
    exp_logits = (xt @ w_route_exp).astype(jnp.float32).reshape(n_tok, N_GROUPS, EXPERTS_PER_GROUP)
    in_grp = jnp.take_along_axis(exp_logits, g_idx[:, :, None], axis=1)[:, 0]
    top_pe, e_local = lax.top_k(jax.nn.softmax(in_grp, axis=-1), EXPERT_TOPK)
    gates = top_pe / jnp.sum(top_pe, axis=-1, keepdims=True) * top_gp
    e_idx = g_idx * EXPERTS_PER_GROUP + e_local

    m = n_tok * EXPERT_TOPK
    flat_e = e_idx.reshape(m)
    flat_tok = jnp.repeat(jnp.arange(n_tok), EXPERT_TOPK)
    flat_gate = gates.reshape(m)
    order = jnp.argsort(flat_e)
    se = flat_e[order]
    counts = jnp.bincount(flat_e, length=N_EXPERTS)
    pcounts = (counts + MOE_BLOCK - 1) // MOE_BLOCK * MOE_BLOCK
    starts = jnp.cumsum(counts) - counts
    pends = jnp.cumsum(pcounts)
    pstarts = pends - pcounts
    dest = pstarts[se] + jnp.arange(m) - starts[se]
    nb = -(-m // MOE_BLOCK) + N_EXPERTS
    rows = nb * MOE_BLOCK
    tok_buf = jnp.full((rows,), n_tok, jnp.int32).at[dest].set(flat_tok[order])
    gate_buf = jnp.zeros((rows,), jnp.float32).at[dest].set(flat_gate[order])
    blk_e = jnp.minimum(jnp.searchsorted(pends, jnp.arange(nb) * MOE_BLOCK, side='right'),
                        N_EXPERTS - 1)
    x_pad = jnp.concatenate([xt, jnp.zeros((1, D), xt.dtype)], axis=0)
    xs = x_pad[tok_buf].reshape(nb, MOE_BLOCK, D)

    def expert_block(args):
        xb, e = args
        hb = jax.nn.silu(xb @ w_gate[e]) * (xb @ w_up[e])
        return hb @ w_down[e]

    yb = lax.map(expert_block, (xs, blk_e)).reshape(rows, D)
    yb = yb * gate_buf[:, None].astype(yb.dtype)
    out = jnp.zeros((n_tok + 1, D), yb.dtype).at[tok_buf].add(yb)[:n_tok]
    return out.reshape(B, S, D)

def second_inputs(seed: int = 0) -> dict:
    key = jax.random.key(seed)
    ks = jax.random.split(key, 24)
    f32 = jnp.float32
    L, D = DEPTH, D_MODEL
    beta = (8.0 * DEPTH) ** -0.25

    def nrm(k, shape, scale):
        return jax.random.normal(k, shape, f32) * scale

    dt = jnp.exp(jax.random.uniform(ks[10], (L, DN_HEADS), f32, math.log(1e-3), math.log(1e-1)))
    return {
        'x': nrm(ks[0], (BATCH, SEQ, D), 1.0),
        'c': nrm(ks[1], (BATCH, D), 1.0),
        'w_ada': nrm(ks[2], (L, D, 6 * D), 0.1 * D ** -0.5),
        'b_ada': nrm(ks[3], (L, 6 * D), 0.01),
        'w_in': nrm(ks[4], (L, D, N_IN), D ** -0.5),
        'kv_norm_g': 1.0 + nrm(ks[5], (L, KV_LATENT), 0.02),
        'w_uk': nrm(ks[6], (L, ATT_HEADS, KV_LATENT, ATT_HEAD_DIM), KV_LATENT ** -0.5),
        'w_uv': nrm(ks[7], (L, ATT_HEADS, KV_LATENT, ATT_HEAD_DIM), KV_LATENT ** -0.5),
        'conv_w': nrm(ks[8], (L, CONV_WIDTH_2, CONV_CH), CONV_WIDTH_2 ** -0.5),
        'a_log': jnp.log(jax.random.uniform(ks[9], (L, DN_HEADS), f32, 1.0, 16.0)),
        'dt_bias': dt + jnp.log(-jnp.expm1(-dt)),
        'dn_norm_g': 1.0 + nrm(ks[11], (L, DN_DV), 0.02),
        'w_br_att': nrm(ks[12], (L, ATT_Q_COLS, D), ATT_Q_COLS ** -0.5),
        'w_br_dn': nrm(ks[13], (L, DN_V_COLS, D), DN_V_COLS ** -0.5),
        'w_out': nrm(ks[14], (L, D, D), beta * D ** -0.5),
        'w_route_grp': nrm(ks[15], (L, D, N_GROUPS), D ** -0.5),
        'w_route_exp': nrm(ks[16], (L, D, N_EXPERTS), D ** -0.5),
        'w_gate': nrm(ks[17], (L, N_EXPERTS, D, EXPERT_FF), D ** -0.5),
        'w_up': nrm(ks[18], (L, N_EXPERTS, D, EXPERT_FF), D ** -0.5),
        'w_down': nrm(ks[19], (L, N_EXPERTS, EXPERT_FF, D), beta * EXPERT_FF ** -0.5),
        'ln_g': 1.0 + nrm(ks[20], (L, 2, D), 0.02),
        'ln_b': nrm(ks[21], (L, 2, D), 0.02),
    }

def second_block(x, c, w_ada, b_ada, w_in, kv_norm_g, w_uk, w_uv, conv_w, a_log, dt_bias,
              dn_norm_g, w_br_att, w_br_dn, w_out, w_route_grp, w_route_exp, w_gate,
              w_up, w_down, ln_g, ln_b):
    alpha = (2.0 * DEPTH) ** 0.25
    cond = jax.nn.silu(c)
    for l in range(DEPTH):
        mod = cond @ w_ada[l] + b_ada[l]
        sh1, sc1, gt1, sh2, sc2, gt2 = [m[:, None, :] for m in jnp.split(mod, 6, axis=-1)]
        h = x * (1.0 + sc1) + sh1
        y = token_mixer(h, w_in[l], kv_norm_g[l], w_uk[l], w_uv[l], conv_w[l], a_log[l],
                        dt_bias[l], dn_norm_g[l], w_br_att[l], w_br_dn[l], w_out[l])
        x = layer_norm_2(alpha * x + (1.0 + gt1) * y, ln_g[l, 0], ln_b[l, 0])
        h = x * (1.0 + sc2) + sh2
        y = hier_moe(h, w_route_grp[l], w_route_exp[l], w_gate[l], w_up[l], w_down[l])
        x = layer_norm_2(alpha * x + (1.0 + gt2) * y, ln_g[l, 1], ln_b[l, 1])
    return x


def setup_inputs(seed=0):
    out = dict(first_inputs(seed))
    for name, value in second_inputs(seed + 1).items():
        if name != "x":
            out[name + "_2"] = value
    return out


def reference(
    x, positions, norm1_g, w_in, conv_dw_w, conv_dw_b, conv_ln_g, conv_ln_b, w_conv_out,
    b_conv_out, q_norm_g, w_uq, kv_norm_g, w_ukv, w_mla_out, w_out, norm2_g, w_ffn_up, ffn_dw_w,
    ffn_dw_b, w_ffn_down, norm_f_g, c_2, w_ada_2, b_ada_2, w_in_2, kv_norm_g_2, w_uk_2, w_uv_2,
    conv_w_2, a_log_2, dt_bias_2, dn_norm_g_2, w_br_att_2, w_br_dn_2, w_out_2, w_route_grp_2,
    w_route_exp_2, w_gate_2, w_up_2, w_down_2, ln_g_2, ln_b_2,
):
    x = first_block(
        x, positions, norm1_g, w_in, conv_dw_w, conv_dw_b, conv_ln_g, conv_ln_b, w_conv_out,
        b_conv_out, q_norm_g, w_uq, kv_norm_g, w_ukv, w_mla_out, w_out, norm2_g, w_ffn_up,
        ffn_dw_w, ffn_dw_b, w_ffn_down, norm_f_g,
    )
    return second_block(
        x, c_2, w_ada_2, b_ada_2, w_in_2, kv_norm_g_2, w_uk_2, w_uv_2, conv_w_2, a_log_2,
        dt_bias_2, dn_norm_g_2, w_br_att_2, w_br_dn_2, w_out_2, w_route_grp_2, w_route_exp_2,
        w_gate_2, w_up_2, w_down_2, ln_g_2, ln_b_2,
    )


_drawn_inputs = setup_inputs


def setup_inputs(seed=0):
    import zlib

    import numpy as np

    out = dict(_drawn_inputs(seed))
    spreads = {}
    factors = {'norm1_g': 4.662,
     'conv_dw_b': 3.056,
     'conv_ln_g': 4.217,
     'conv_ln_b': 4.872,
     'b_conv_out': 3.364,
     'q_norm_g': 8.0,
     'kv_norm_g': 8.0,
     'norm2_g': 3.224,
     'ffn_dw_b': 3.06,
     'b_ada_2': 3.941,
     'kv_norm_g_2': 8.0,
     'dn_norm_g_2': 26.552}
    for name, (base, spread) in spreads.items():
        noise = np.random.default_rng([zlib.crc32(name.encode()), seed]).standard_normal(out[name].shape)
        drawn = base * np.exp(spread * noise) if base else spread * noise
        out[name] = jnp.asarray(drawn.astype(out[name].dtype))
    for name, factor in factors.items():
        out[name] = (out[name] * factor).astype(out[name].dtype)
    return out
```

```python
from contextlib import ExitStack

import numpy as np

import concourse.bass as bass
from concourse import mybir

ACT = mybir.ActivationFunctionType
ALU = mybir.AluOpType
AX = mybir.AxisListType
F32 = mybir.dt.float32
I32 = mybir.dt.int32
U32 = mybir.dt.uint32

P = 128
S = 512
TT = S // P
D = 1024
DT = D // P
CW, CK = 512, 31
CT = CW // P
HPAD = CK // 2
H1, NOPE, ROPE, VD = 8, 64, 32, 64
QR, KVR = 384, 256
FF = 2816
FT = FF // P
RING = 4
CHUNK = 32
BANKS = 8
EPS = 1e-6
TWO_PI = 2.0 * np.pi


class Plan:

    def __init__(self):
        self.blocks = []
        self.jobs = []
        self.number = {}
        self.emptied = {}
        self.count = {"act": 0, "dve": 0}
        self.first = {}
        self.last_user = {}

    def weights(self, blocks):
        at = len(self.blocks)
        self.blocks += blocks
        return at

    def align(self, n):
        while len(self.blocks) % CHUNK + n > CHUNK:
            self.blocks.append(None)

    def job(self, name, i, engine, blocks=None, shared=None):
        n = len(self.jobs)
        self.jobs.append((name, i, engine))
        self.number[name, i] = n
        self.count[engine] += 1
        self.emptied[name, i] = (engine, self.count[engine])
        if blocks is not None:
            at, many = self.weights(blocks), len(blocks)
        elif shared is not None:
            at, many = shared
        else:
            return
        self.first[name, i] = at
        for c in range(at // CHUNK, (at + many - 1) // CHUNK + 1):
            self.last_user[c] = n


def column_blocks(weight, rows, cols):
    return [(weight, k, cols) for k in range(rows // P)]


def span(a, n=P):
    return ("cols", a, n)


def make_plan():
    p = Plan()
    plan_first(p)
    plan_second(p)
    while len(p.blocks) % CHUNK:
        p.blocks.append(None)
    return p


def plan_first(p):
    kr = 2 * CW + QR + KVR
    g0 = kr + ROPE
    p.job("ss1", 0, "act")
    for t in range(CT):
        p.job("cgate", t, "act", column_blocks("w_in", D, span(CW + t * P)))
        p.job("cval", t, "dve", column_blocks("w_in", D, span(t * P)))
    for t in range(QR // P):
        p.job("qc", t, "act", column_blocks("w_in", D, span(2 * CW + t * P)))
    for t in range(KVR // P):
        p.job("kvc", t, "act", column_blocks("w_in", D, span(2 * CW + QR + t * P)))
    p.job("kr", 0, "dve", column_blocks("w_in", D, ("rope", None, kr)))
    p.job("ssq", 0, "act")
    p.job("sskv", 0, "act")
    for h in range(H1):
        base = h * (NOPE + ROPE)
        p.job("uq", h, "dve", column_blocks("w_uq", QR, ("rope", base, base + NOPE)))
    for i in range(H1 // 2):
        p.job("uk", i, "act", column_blocks("w_ukv", KVR, ("pair", 2 * i * P, (2 * i + 1) * P)))
    p.align(8)
    v = p.weights([("w_ukv", k, ("v", c)) for k in range(KVR // P) for c in range(4)])
    for t in range(TT):
        p.job("v", t, "act", shared=(v, 8))
    n = H1 * TT
    for i in range(n + 2):
        if i < n:
            p.job("sc", i, "act")
        if 1 <= i <= n:
            p.job("pt", i - 1, "act" if i % 2 else "dve")
        if i >= 2:
            p.job("pv", i - 2, "dve")
    for t in range(TT):
        p.job("ot", t, "act")
    p.job("cmean", 0, "act")
    p.job("cvar", 0, "act")
    for t in range(DT):
        p.job("g1", t, "act", column_blocks("w_in", D, span(g0 + t * P)))
        p.job("co", t, "dve", column_blocks("w_conv_out", CW, span(t * P)))
        p.job("g2", t, "act", column_blocks("w_in", D, span(g0 + D + t * P)))
        p.job("mo", t, "dve", column_blocks("w_mla_out", H1 * VD, span(t * P)))
    for t in range(DT):
        p.job("wo", t, "dve", column_blocks("w_out", D, span(t * P)))
    p.job("ss2", 0, "act")
    for t in range(FT):
        p.job("fg", t, "dve", column_blocks("w_ffn_up", D, span(t * P)))
        p.job("fu", t, "dve", column_blocks("w_ffn_up", D, span(FF + t * P)))
    for t in range(DT):
        p.job("fd", t, "dve", column_blocks("w_ffn_down", FF, span(t * P)))
    p.job("ssf", 0, "act")


def block_array(inputs, block):
    out = np.zeros((P, P), np.float32)
    if block is None:
        return out
    name, k, cols = block
    w = inputs[name]
    w = w.reshape(-1, w.shape[-1])[k * P:(k + 1) * P]
    kind = cols[0]
    if kind == "cols":
        c = w[:, cols[1]:cols[1] + cols[2]]
        out[:, :c.shape[1]] = c
    elif kind == "rope":
        if cols[1] is not None:
            out[:, :NOPE] = w[:, cols[1]:cols[1] + NOPE]
        r, h = cols[2], ROPE // 2
        out[:, 64:96] = w[:, r:r + ROPE]
        out[:, 96:96 + h] = w[:, r + h:r + ROPE]
        out[:, 96 + h:] = w[:, r:r + h]
    elif kind == "pair":
        out[:, :64] = w[:, cols[1]:cols[1] + 64]
        out[:, 64:] = w[:, cols[2]:cols[2] + 64]
    elif kind == "head" or kind == "route":
        out[:, :w.shape[1]] = w
    elif kind == "small":
        for j, at in enumerate((C_WI, C_A, C_B)):
            out[:, 8 * j:8 * j + 8] = w[:, at:at + 8]
    elif kind == "v":
        for j in range(2):
            h = 2 * cols[1] + j
            out[:, 64 * j:64 * j + 64] = w[:, h * P + 64:h * P + P]
    return out


def experts_array(inputs):
    out = np.zeros((NE, 3, P, CHUNK * P), np.float32)
    for i, (name, tiles) in enumerate((("w_gate_2", 8), ("w_up_2", 8), ("w_down_2", 4))):
        w = inputs[name][0]
        out[:, i] = w.reshape(NE, tiles, P, -1).transpose(0, 2, 1, 3).reshape(NE, P, -1)
    return out


def stream_array(inputs, plan):
    n = len(plan.blocks) // CHUNK
    out = np.zeros((n, P, CHUNK, P), np.float32)
    for i, b in enumerate(plan.blocks):
        if b is not None:
            out[i // CHUNK, :, i % CHUNK] = block_array(inputs, b)
    return out.reshape(n, P, CHUNK * P)


def columns(a, tiles):
    return a.reshape(tiles, P).T


VECS = {}


def vec_layout():
    at = 0
    for name, n in (("norm1_g", 8), ("conv_dw_w", CT * CK), ("conv_dw_b", CT), ("conv_ln_g", CT),
                    ("conv_ln_b", CT), ("b_conv_out", 8), ("q_norm_g", 3), ("kv_norm_g", 2),
                    ("norm2_g", 8), ("ffn_dw_w", 2 * FT * 3), ("ffn_dw_b", 2 * FT),
                    ("norm_f_g", 8), ("freq", 1), ("phase", 1), ("turn", 1),
                    ("b_ada_2", 48), ("kv_norm_g_2", 2), ("conv_w_2", 24 * 4),
                    ("dn_norm_g_2", 1), ("ln_g_2", 8), ("ln_b_2", 8)):
        VECS[name] = (at, n)
        at += n
    return at


NVEC = vec_layout()


def vec_array(inputs):
    out = np.zeros((P, NVEC), np.float32)

    def put(name, a):
        at, n = VECS[name]
        out[:, at:at + n] = a

    def flat(name):
        return inputs[name].reshape(inputs[name].shape[-1])

    for name, n in (("norm1_g", 8), ("conv_dw_b", CT), ("conv_ln_g", CT), ("conv_ln_b", CT),
                    ("b_conv_out", 8), ("q_norm_g", 3), ("kv_norm_g", 2), ("norm2_g", 8),
                    ("ffn_dw_b", 2 * FT), ("norm_f_g", 8), ("b_ada_2", 48), ("kv_norm_g_2", 2),
                    ("dn_norm_g_2", 1)):
        put(name, columns(flat(name), n))
    put("conv_dw_w", inputs["conv_dw_w"][0].reshape(CK, CT, P).transpose(2, 1, 0).reshape(P, -1))
    put("ffn_dw_w", inputs["ffn_dw_w"][0].reshape(3, 2 * FT, P).transpose(2, 1, 0).reshape(P, -1))
    put("conv_w_2", inputs["conv_w_2"][0].reshape(4, 24, P).transpose(2, 1, 0).reshape(P, -1))
    put("ln_g_2", columns(inputs["ln_g_2"][0, 0], 8))
    put("ln_b_2", columns(inputs["ln_b_2"][0, 0], 8))
    j = np.arange(P) % (ROPE // 2)
    freq = 1.0 / (np.float32(10000.0) ** (np.arange(0, ROPE, 2, dtype=np.float32) / ROPE))
    put("freq", freq.astype(np.float32)[j][:, None])
    row = np.arange(P)
    turn = np.where(row < 96, 0.25, np.where(row < 112, 0.5, 0.0))
    put("phase", (turn * TWO_PI).astype(np.float32)[:, None])
    put("turn", turn.astype(np.float32)[:, None])
    return out


class Core:

    def __init__(self, nc, ctx, plan, args):
        self.nc, self.ctx, self.plan, self.args = nc, ctx, plan, args
        self.sems = {}
        self.given = {"act": 0, "dve": 0}
        self.ps = ctx.enter_context(nc.psum_tensor("banks", [P, BANKS, 512], F32))
        self.ring = self.sb("ring", [P, RING, CHUNK * P])
        self.ident = self.sb("ident", [P, P])
        self.ones = self.sb("ones", [P, P])
        self.vecs = self.sb("vecs", [P, NVEC])
        self.cons = self.sb("cons", [P, 4])
        self.arena = self.sb("arena", [P, ARENA])
        self.small = self.sb("small", [P, SMALL])
        self.mod = self.sb("modulation", [P, MOD_TILES])
        self.route = self.view(RT_, ROUTE)
        rows = nc.dram_tensor("expert_rows", [NB * SLOTS, D], F32, kind="Internal").ap()
        results = nc.dram_tensor("expert_results", [NB * SLOTS, D], F32, kind="Internal").ap()
        self.y_spill = nc.dram_tensor("attention_result", [P, DT, S], F32, kind="Internal").ap()
        self.xs_rows, self.y_rows = rows, results
        self.xs_blocks = rows.rearrange("(b p) n -> b p n", p=SLOTS)
        self.y_blocks = results.rearrange("(b p) n -> b p n", p=SLOTS)

    def sb(self, name, shape, dt=F32):
        return self.ctx.enter_context(self.nc.sbuf_tensor(name, shape, dt))

    def sem(self, name):
        if name not in self.sems:
            self.sems[name] = self.ctx.enter_context(self.nc.semaphore(name))
        return self.sems[name]

    def vec(self, name, i=0):
        at = VECS[name][0] + i
        return self.vecs[:, at:at + 1]

    def view(self, at, *shape):
        n = int(np.prod(shape))
        assert at + n <= ARENA, (at, n)
        v = self.arena[:, at:at + n]
        if len(shape) == 2:
            return v.rearrange("p (a b) -> p a b", a=shape[0])
        if len(shape) == 3:
            return v.rearrange("p (a b c) -> p a b c", a=shape[0], b=shape[1])
        return v

    def bank(self, name, i):
        return self.ps[:, self.plan.number[name, i] % BANKS, :]

    def reused(self, name, i):
        return self.plan.number[name, i] >= BANKS

    def bank_free(self, name, i):
        return self.put_away(*self.plan.jobs[self.plan.number[name, i] - BANKS][:2])

    def finished(self, name, i):
        return self.sem("job_done"), self.plan.number[name, i] + 1

    def put_away(self, name, i):
        who, value = self.plan.emptied[name, i]
        return self.sem("emptied_" + who), value

    def landed(self, at):
        n = at // CHUNK
        return self.sem(f"weights{n % RING}"), 16 * (n // RING + 1)

    def weight(self, at, n=1):
        o = at % CHUNK * P
        return self.ring[:, at // CHUNK % RING, o:o + n * P]

    def emptied(self, who, name, i):
        self.given[who] += 1
        assert self.plan.emptied[name, i] == (who, self.given[who]), (name, i, who)
        return self.sem("emptied_" + who)


ARENA = 34936 + 64
X_, H_, BIG_ = 0, 4096, 8192
U_ = BIG_ + FT * S
CV_ = U_ + CT * (S + CK - 1)
C_ = CV_ + CT * S
SQ_ = C_ + 3072
RS_ = SQ_ + 4 * S
TAB_ = RS_ + S
TMP_ = TAB_ + S
O_ = TMP_ + 6 * S
SM_ = O_ + 2048


def load_weights(c, sp):
    for n in range(len(c.plan.blocks) // CHUNK):
        if n >= RING:
            sp.wait_ge(c.sem("job_done"), c.plan.last_user[n - RING] + 1)
        sp.dma_start(c.ring[:, n % RING, :], c.args["stream"][n]).then_inc(c.sem(f"weights{n % RING}"), 16)


def first_pe(c, pe):
    x, h = c.view(X_, DT, S), c.view(H_, DT, S)
    qn, kvn = c.view(C_, 3, S), c.view(C_ + 3 * S, 2, S)
    qT, kT, v = c.view(BIG_, H1, S), c.view(BIG_ + 4096, H1, S), c.view(BIG_ + 8192, TT, S)
    sq = c.view(SQ_, 4, S)
    prob, probT = c.view(TMP_, 2, S), c.view(TMP_ + 2 * S, 2, TT, P)
    o, oT = c.view(O_, TT, S), c.view(C_, TT, S)
    cv, mg, act = c.view(CV_, CT, S), c.view(BIG_, DT, S), c.view(BIG_, FT, S)
    sq_used = c.sem("squares_used")
    squares = [0, 0]

    def gemm(name, i, rhs, tiles):
        if c.reused(name, i):
            pe.wait_ge(*c.bank_free(name, i))
        bank, at = c.bank(name, i), c.plan.first[name, i]
        for k in range(tiles):
            if k == 0 or (at + k) % CHUNK == 0:
                pe.wait_ge(*c.landed(at + k))
            m = pe.matmul(bank, c.weight(at + k), rhs(k), start=k == 0, stop=k == tiles - 1)
        m.then_inc(c.sem("job_done"), 1)

    def column_sums(name, tiles, counted="squares"):
        if c.reused(name, 0):
            pe.wait_ge(*c.bank_free(name, 0))
        bank = c.bank(name, 0)
        for k in range(tiles):
            squares[0] += 1
            pe.wait_ge(c.sem(counted), squares[0])
            m = pe.matmul(bank, c.ones[:, :], sq[:, k % 4, :], start=k == 0, stop=k == tiles - 1)
            m.then_inc(c.sem("job_done") if k == tiles - 1 else sq_used, 1)

    pe.wait_ge(c.sem("constants"), 2)
    column_sums("ss1", DT)
    pe.wait_ge(c.sem("h1"), DT)
    for t in range(CT):
        gemm("cgate", t, lambda k: h[:, k, :], DT)
        gemm("cval", t, lambda k: h[:, k, :], DT)
    for t in range(3):
        gemm("qc", t, lambda k: h[:, k, :], DT)
    for t in range(2):
        gemm("kvc", t, lambda k: h[:, k, :], DT)
    gemm("kr", 0, lambda k: h[:, k, :], DT)
    column_sums("ssq", 3)
    column_sums("sskv", 2)
    pe.wait_ge(c.sem("qn"), 3)
    for i in range(H1):
        gemm("uq", i, lambda k: qn[:, k, :], 3)
    pe.wait_ge(c.sem("kvn"), 2)
    for i in range(H1 // 2):
        gemm("uk", i, lambda k: kvn[:, k, :], 2)
    for t in range(TT):
        pe.wait_ge(*c.bank_free("v", t))
        bank = c.bank("v", t)
        pe.wait_ge(*c.landed(c.plan.first["v", t]))
        for k in range(2):
            m = pe.matmul(bank, kvn[:, k, t * P:(t + 1) * P],
                          c.weight(c.plan.first["v", t] + 4 * k, 4), start=k == 0, stop=k == 1)
        m.then_inc(c.sem("job_done"), 1)
    n = H1 * TT
    pe.wait_ge(c.sem("kr_spread"), H1)
    pe.wait_ge(*c.put_away("v", TT - 1))
    for i in range(n + 2):
        if i < n:
            hd, t = i // TT, i % TT
            pe.wait_ge(*c.bank_free("sc", i))
            bank = c.bank("sc", i)
            pe.wait_ge(*c.put_away("uq", hd))
            pe.wait_ge(*c.put_away("uk", hd // 2))
            pe.matmul(bank, qT[0:96, hd, t * P:(t + 1) * P], kT[0:96, hd, :], start=True, stop=True) \
                .then_inc(c.sem("job_done"), 1)
        if 1 <= i <= n:
            pe.wait_ge(*c.bank_free("pt", i - 1))
            bank = c.bank("pt", i - 1)
            pe.wait_ge(*c.put_away("sc", i - 1))
            for k in range(TT):
                m = pe.transpose(bank[:, k * P:(k + 1) * P], prob[:, (i - 1) % 2, k * P:(k + 1) * P], c.ident[:, :])
            m.then_inc(c.sem("job_done"), 1)
        if i >= 2:
            j = i - 2
            hd = j // TT
            pe.wait_ge(*c.bank_free("pv", j))
            bank = c.bank("pv", j)
            pe.wait_ge(*c.put_away("pt", j))
            for k in range(TT):
                m = pe.matmul(bank[:, 0:VD], probT[:, j % 2, k, :], v[:, k, hd * VD:(hd + 1) * VD],
                              start=k == 0, stop=k == TT - 1)
            m.then_inc(c.sem("job_done"), 1)
    for t in range(TT):
        pe.wait_ge(*c.bank_free("ot", t))
        bank = c.bank("ot", t)
        pe.wait_ge(*c.put_away("pv", n - TT + t))
        for j in range(TT):
            m = pe.transpose(bank[:, j * P:(j + 1) * P], o[:, t, j * P:(j + 1) * P], c.ident[:, :])
        m.then_inc(c.sem("job_done"), 1)
    pe.wait_ge(*c.bank_free("cmean", 0))
    bank = c.bank("cmean", 0)
    pe.wait_ge(c.sem("conv"), CT)
    for k in range(CT):
        m = pe.matmul(bank, c.ones[:, :], cv[:, k, :], start=k == 0, stop=k == CT - 1)
    m.then_inc(c.sem("job_done"), 1)
    column_sums("cvar", CT)
    for t in range(DT):
        gemm("g1", t, lambda k: h[:, k, :], DT)
        pe.wait_ge(c.sem("cn"), CT)
        gemm("co", t, lambda k: cv[:, k, :], CT)
        gemm("g2", t, lambda k: h[:, k, :], DT)
        pe.wait_ge(*c.put_away("ot", TT - 1))
        gemm("mo", t, lambda k: oT[:, k, :], TT)
    pe.wait_ge(*c.put_away("mo", DT - 1))
    for t in range(DT):
        gemm("wo", t, lambda k: mg[:, k, :], DT)
    column_sums("ss2", DT)
    pe.wait_ge(c.sem("h2"), DT)
    for t in range(FT):
        gemm("fg", t, lambda k: h[:, k, :], DT)
        gemm("fu", t, lambda k: h[:, k, :], DT)
    pe.wait_ge(c.sem("act"), FT)
    for t in range(DT):
        gemm("fd", t, lambda k: act[:, k, :], FT)
    column_sums("ssf", DT)


def first_act(c, a):
    x, h = c.view(X_, DT, S), c.view(H_, DT, S)
    qc, kvc, kr = c.view(C_, 3, S), c.view(C_ + 3 * S, 2, S), c.view(C_ + 5 * S, S)
    qT, kT, v = c.view(BIG_, H1, S), c.view(BIG_ + 4096, H1, S), c.view(BIG_ + 8192, TT, S)
    sq, tmp, rstd = c.view(SQ_, 4, S), c.view(TMP_, 6, S), c.view(RS_, S)
    prob, probT = c.view(TMP_, 2, S), c.view(TMP_ + 2 * S, 2, S)
    o, oT, cv = c.view(O_, TT, S), c.view(C_, TT, S), c.view(CV_, CT, S)
    nmax, rsum = c.view(SM_, 4), c.view(SM_ + 4, 4)
    eps = c.cons[:, 0:1]
    used = [0]

    def squares(source, tiles, before=lambda k: None):
        for k in range(tiles):
            before(k)
            if k >= 4:
                used[0] += 1
                a.wait_ge(c.sem("squares_used"), used[0])
            a.activation(sq[:, k % 4, :], source(k), ACT.Square).then_inc(c.sem("squares"), 1)
        used[0] += tiles - 1 - max(tiles - 4, 0)

    def root(name, width, out=None):
        a.wait_ge(*c.finished(name, 0))
        bank = c.bank(name, 0)
        a.activation(rstd if out is None else out, bank, ACT.Sqrt, bias=eps, scale=1.0 / width) \
            .then_inc(c.emptied("act", name, 0), 1)

    a.wait_ge(c.sem("vectors"), 16)
    a.wait_ge(c.sem("constants"), 2)
    for k in range(2):
        a.wait_ge(c.sem(f"x{k}"), 16)
    squares(lambda k: x[:, k, :], DT)
    a.wait_ge(c.sem("angle"), 1)
    a.activation(c.view(TAB_, S)[64:P], c.view(TAB_, S)[64:P], ACT.Sin).then_inc(c.sem("table"), 1)
    root("ss1", D)
    for t in range(CT):
        a.wait_ge(*c.finished("cgate", t))
        bank = c.bank("cgate", t)
        if t >= 2:
            a.wait_ge(*c.put_away("cval", t - 2))
        a.activation(tmp[:, t % 2, :], bank, ACT.Sigmoid).then_inc(c.emptied("act", "cgate", t), 1)
    for t in range(3):
        a.wait_ge(*c.finished("qc", t))
        bank = c.bank("qc", t)
        a.activation(sq[:, t, :], bank, ACT.Square).then_inc(c.sem("squares"), 1)
        a.activation(qc[:, t, :], bank, ACT.Copy).then_inc(c.emptied("act", "qc", t), 1)
    used[0] += 2
    a.wait_ge(*c.finished("ssq", 0))
    for t in range(2):
        a.wait_ge(*c.finished("kvc", t))
        bank = c.bank("kvc", t)
        a.activation(sq[:, t, :], bank, ACT.Square).then_inc(c.sem("squares"), 1)
        a.activation(kvc[:, t, :], bank, ACT.Copy).then_inc(c.emptied("act", "kvc", t), 1)
    used[0] += 1
    a.wait_ge(c.sem("h1"), DT)
    root("ssq", QR)
    root("sskv", KVR, c.view(TMP_ + 2 * S, S))
    for i in range(H1):
        a.wait_ge(*c.finished("uq", i))
        bank = c.bank("uq", i)
        a.activation(qT[0:NOPE, i, :], bank[0:NOPE], ACT.Copy, scale=(NOPE + ROPE) ** -0.5) \
            .then_inc(c.sem("q_plain"), 1)
    for i in range(H1 // 2):
        a.wait_ge(*c.finished("uk", i))
        bank = c.bank("uk", i)
        a.activation(kT[0:NOPE, 2 * i, :], bank[0:64], ACT.Copy)
        a.activation(kT[0:NOPE, 2 * i + 1, :], bank[64:P], ACT.Copy).then_inc(c.emptied("act", "uk", i), 1)
    for t in range(TT):
        a.wait_ge(*c.finished("v", t))
        bank = c.bank("v", t)
        a.activation(v[:, t, :], bank, ACT.Copy).then_inc(c.emptied("act", "v", t), 1)
    for rows in (c.xs_blocks, c.y_blocks):
        a.dma_start(rows, c.args["zeros"].to_broadcast([NB, SLOTS, D])).then_inc(c.sem("zeroed"), 16)
    n = H1 * TT
    a.wait_ge(c.sem("kvn"), 2)
    for i in range(n + 1):
        if i < n:
            a.wait_ge(*c.finished("sc", i))
            bank = c.bank("sc", i)
            a.wait_ge(c.sem("nmax"), i + 1)
            if i >= 2:
                a.wait_ge(*c.finished("pt", i - 2))
            a.activation(prob[:, i % 2, :], bank, ACT.Exp, bias=nmax[:, i % 4:i % 4 + 1],
                         accum_out=rsum[:, i % 4:i % 4 + 1]).then_inc(c.emptied("act", "sc", i), 1)
        if i >= 1 and i % 2:
            j = i - 1
            a.wait_ge(*c.finished("pt", j))
            bank = c.bank("pt", j)
            if j >= 2:
                a.wait_ge(*c.finished("pv", j - 2))
            a.activation(probT[:, j % 2, :], bank, ACT.Copy).then_inc(c.emptied("act", "pt", j), 1)
    for t in range(TT):
        a.wait_ge(*c.finished("ot", t))
        bank = c.bank("ot", t)
        a.activation(oT[:, :, t * P:(t + 1) * P], bank.rearrange("p (j q) -> p j q", j=TT), ACT.Copy) \
            .then_inc(c.emptied("act", "ot", t), 1)
    a.wait_ge(*c.finished("cmean", 0))
    bank = c.bank("cmean", 0)
    a.activation(tmp[:, 4, :], bank, ACT.Copy, scale=1.0 / CW).then_inc(c.emptied("act", "cmean", 0), 1)
    squares(lambda k: cv[:, k, :], CT, lambda k: a.wait_ge(c.sem("centred"), k + 1))
    root("cvar", CW)
    for k in range(CT):
        a.wait_ge(c.sem("scaled"), k + 1)
        a.activation(cv[:, k, :], cv[:, k, :], ACT.Silu, bias=c.vec("conv_ln_b", k), scale=c.vec("conv_ln_g", k)) \
            .then_inc(c.sem("cn"), 1)
    for t in range(DT):
        a.wait_ge(*c.finished("g1", t))
        bank = c.bank("g1", t)
        if t >= 2:
            a.wait_ge(*c.put_away("co", t - 2))
        a.activation(tmp[:, t % 2, :], bank, ACT.Sigmoid).then_inc(c.emptied("act", "g1", t), 1)
        a.wait_ge(*c.finished("g2", t))
        bank = c.bank("g2", t)
        if t >= 2:
            a.wait_ge(*c.put_away("mo", t - 2))
        a.activation(tmp[:, 2 + t % 2, :], bank, ACT.Sigmoid).then_inc(c.emptied("act", "g2", t), 1)
    modulation_act(c, a)
    squares(lambda k: x[:, k, :], DT, lambda k: a.wait_ge(*c.put_away("wo", k)))
    a.wait_ge(c.sem("scaled"), CT)
    root("ss2", D)
    for t in range(FT):
        for j, name in enumerate(("fg", "fu")):
            f = t + j * FT
            a.wait_ge(*c.finished(name, t))
            bank = c.bank(name, t)
            if t >= 2:
                a.wait_ge(c.sem("act"), t - 1)
            w = VECS["ffn_dw_w"][0] + 3 * f
            a.activation(tmp[:, 2 * (t % 2) + j, :], bank, ACT.Identity, bias=c.vec("ffn_dw_b", f),
                         scale=c.vecs[:, w + 1:w + 2]).then_inc(c.sem("middle_tap"), 1)
        a.wait_ge(*c.put_away("fg", t))
        a.activation(tmp[:, 2 * (t % 2), :], tmp[:, 2 * (t % 2), :], ACT.Silu).then_inc(c.sem("gate_silu"), 1)
    squares(lambda k: x[:, k, :], DT, lambda k: a.wait_ge(*c.put_away("fd", k)))
    a.wait_ge(c.sem("h2"), DT)
    root("ssf", D)


def first_dve(c, v):
    x, h = c.view(X_, DT, S), c.view(H_, DT, S)
    qc, kvc, kr = c.view(C_, 3, S), c.view(C_ + 3 * S, 2, S), c.view(C_ + 5 * S, S)
    qT = c.view(BIG_, H1, S)
    u, cv = c.view(U_, CT, S + CK - 1), c.view(CV_, CT, S)
    tmp, rstd, tab = c.view(TMP_, 6, S), c.view(RS_, S), c.view(TAB_, S)
    rstd_kv = c.view(TMP_ + 2 * S, S)
    probT, o = c.view(TMP_ + 2 * S, 2, S), c.view(O_, TT, S)
    mg, act = c.view(BIG_, DT, S), c.view(BIG_, FT, S)
    nmax, rsum, rinv = c.view(SM_, 4), c.view(SM_ + 4, 4), c.view(SM_ + 8, 4)

    def rows_times_root(out, source, gain, tiles, name, root):
        for k in range(tiles):
            v.scalar_tensor_tensor(out[:, k, :], source[:, k, :], c.vec(gain, k), root, ALU.mult, ALU.mult) \
                .then_inc(c.sem(name), 1)

    v.wait_ge(c.sem("vectors"), 16)
    v.wait_ge(c.sem("positions"), 16)
    ang, turns = tmp[64:P, 0, :], tmp[64:P, 1, :]
    v.tensor_copy(turns, c.view(TMP_ + 2 * S, S)[64:P].bitcast(I32))
    v.drain()
    v.tensor_scalar(ang, turns, c.vec("freq")[64:P], None, ALU.mult)
    v.drain()
    v.tensor_scalar(turns, ang, 1.0 / TWO_PI, c.vec("turn")[64:P], ALU.mult, ALU.add)
    v.drain()
    v.tensor_scalar(turns, turns, 12582912.0, None, ALU.add)
    v.drain()
    v.tensor_scalar(turns, turns, -12582912.0, None, ALU.add)
    v.drain()
    for part in (6.28125, 0.0019340515136718750, 1.2556138e-6):
        v.scalar_tensor_tensor(ang, turns, -part, ang, ALU.mult, ALU.add)
        v.drain()
    v.tensor_scalar(ang, ang, c.vec("phase")[64:P], float(np.float32(3.1415925)), ALU.add, ALU.min)
    v.drain()
    v.tensor_scalar(tab[64:P], ang, -float(np.float32(3.1415925)), None, ALU.max).then_inc(c.sem("angle"), 1)
    v.wait_ge(c.sem("x0"), 16)
    v.wait_ge(c.sem("x1"), 16)
    v.wait_ge(*c.put_away("ss1", 0))
    v.reciprocal(rstd, rstd)
    v.drain()
    rows_times_root(h, x, "norm1_g", DT, "h1", rstd)
    v.wait_ge(c.sem("pads"), 1)
    for t in range(CT):
        v.wait_ge(*c.finished("cval", t))
        bank = c.bank("cval", t)
        v.wait_ge(*c.put_away("cgate", t))
        v.tensor_tensor(u[:, t, HPAD:HPAD + S], bank, tmp[:, t % 2, :], ALU.mult) \
            .then_inc(c.emptied("dve", "cval", t), 1)
    v.drain()

    def conv_taps():
        for j in range(CK):
            for t in range(CT):
                w = VECS["conv_dw_w"][0] + t * CK + j
                w = c.vecs[:, w:w + 1]
                if j == 0:
                    v.tensor_scalar(cv[:, t, :], u[:, t, 0:S], w, c.vec("conv_dw_b", t), ALU.mult, ALU.add)
                else:
                    m = v.scalar_tensor_tensor(cv[:, t, :], u[:, t, j:j + S], w, cv[:, t, :], ALU.mult, ALU.add)
                    if j == CK - 1:
                        m.then_inc(c.sem("conv"), 1)
            v.drain()
            yield

    taps = conv_taps()

    def rotate(bank, out, scale):
        v.scalar_tensor_tensor(out[64:96], bank[64:96], scale, tab[64:96], ALU.mult, ALU.mult)
        m = v.scalar_tensor_tensor(tmp[64:96, 5, :], bank[96:P], scale, tab[96:P], ALU.mult, ALU.mult)
        return m

    for _ in range(12):
        next(taps)
    v.wait_ge(c.sem("table"), 1)
    v.wait_ge(*c.finished("kr", 0))
    bank = c.bank("kr", 0)
    rotate(bank, kr, 1.0).then_inc(c.emptied("dve", "kr", 0), 1)
    v.drain()
    v.tensor_tensor(kr[64:96], kr[64:96], tmp[64:96, 5, :], ALU.add).then_inc(c.sem("kr_turned"), 1)
    v.wait_ge(*c.put_away("ssq", 0))
    v.reciprocal(rstd, rstd)
    v.drain()
    rows_times_root(qc, qc, "q_norm_g", 3, "qn", rstd)
    v.wait_ge(*c.put_away("sskv", 0))
    v.reciprocal(rstd_kv, rstd_kv)
    v.drain()
    rows_times_root(kvc, kvc, "kv_norm_g", 2, "kvn", rstd_kv)
    for i in range(H1):
        v.wait_ge(*c.finished("uq", i))
        bank = c.bank("uq", i)
        v.wait_ge(c.sem("q_plain"), i + 1)
        rotate(bank, qT[:, i, :], (NOPE + ROPE) ** -0.5)
        v.drain()
        v.tensor_tensor(qT[64:96, i, :], qT[64:96, i, :], tmp[64:96, 5, :], ALU.add) \
            .then_inc(c.emptied("dve", "uq", i), 1)
        v.drain()
        next(taps)
    n = H1 * TT
    for i in range(n + 2):
        if i < n:
            v.wait_ge(*c.finished("sc", i))
            bank = c.bank("sc", i)
            v.tensor_reduce(nmax[:, i % 4:i % 4 + 1], bank, AX.X, ALU.max, negate=True).then_inc(c.sem("nmax"), 1)
        if 1 <= i <= n and i % 2 == 0:
            j = i - 1
            v.wait_ge(*c.finished("pt", j))
            bank = c.bank("pt", j)
            if j >= 2:
                v.wait_ge(*c.finished("pv", j - 2))
            v.tensor_copy(probT[:, j % 2, :], bank).then_inc(c.emptied("dve", "pt", j), 1)
        if i >= 2:
            j = i - 2
            hd, t = j // TT, j % TT
            v.wait_ge(*c.put_away("sc", j))
            v.reciprocal(rinv[:, j % 4:j % 4 + 1], rsum[:, j % 4:j % 4 + 1])
            v.drain()
            v.wait_ge(*c.finished("pv", j))
            bank = c.bank("pv", j)
            v.tensor_scalar(o[:, t, hd * VD:(hd + 1) * VD], bank[:, 0:VD], rinv[:, j % 4:j % 4 + 1], None, ALU.mult) \
                .then_inc(c.emptied("dve", "pv", j), 1)
        if i % 2 == 0:
            next(taps, None)
    for _ in taps:
        pass
    v.wait_ge(*c.put_away("cmean", 0))
    for k in range(CT):
        v.tensor_tensor(cv[:, k, :], cv[:, k, :], tmp[:, 4, :], ALU.subtract).then_inc(c.sem("centred"), 1)
    v.wait_ge(*c.put_away("cvar", 0))
    v.reciprocal(rstd, rstd)
    v.drain()
    for k in range(CT):
        v.tensor_tensor(cv[:, k, :], cv[:, k, :], rstd, ALU.mult).then_inc(c.sem("scaled"), 1)
    v.wait_ge(*c.put_away("ot", TT - 1))
    for t in range(DT):
        v.wait_ge(*c.finished("co", t))
        bank = c.bank("co", t)
        v.wait_ge(*c.put_away("g1", t))
        v.scalar_tensor_tensor(mg[:, t, :], bank, c.vec("b_conv_out", t), tmp[:, t % 2, :], ALU.add, ALU.mult) \
            .then_inc(c.emptied("dve", "co", t), 1)
        v.wait_ge(*c.finished("mo", t))
        bank = c.bank("mo", t)
        v.wait_ge(*c.put_away("g2", t))
        v.tensor_tensor(tmp[:, 4, :], bank, tmp[:, 2 + t % 2, :], ALU.mult)
        v.drain()
        v.tensor_tensor(mg[:, t, :], mg[:, t, :], tmp[:, 4, :], ALU.add).then_inc(c.emptied("dve", "mo", t), 1)
        v.drain()
    for t in range(DT):
        v.wait_ge(*c.finished("wo", t))
        bank = c.bank("wo", t)
        v.tensor_tensor(x[:, t, :], x[:, t, :], bank, ALU.add).then_inc(c.emptied("dve", "wo", t), 1)
    v.wait_ge(*c.put_away("ss2", 0))
    v.reciprocal(rstd, rstd)
    v.drain()
    rows_times_root(h, x, "norm2_g", DT, "h2", rstd)
    ada = modulation(c, v)
    for t in range(FT):
        for j, name in enumerate(("fg", "fu")):
            f = t + j * FT
            w = VECS["ffn_dw_w"][0] + 3 * f
            out = tmp[:, 2 * (t % 2) + j, :]
            v.wait_ge(*c.finished(name, t))
            bank = c.bank(name, t)
            v.wait_ge(c.sem("middle_tap"), 2 * t + j + 1)
            v.scalar_tensor_tensor(out[:, 1:S], bank[:, 0:S - 1], c.vecs[:, w:w + 1], out[:, 1:S], ALU.mult, ALU.add)
            v.drain()
            v.scalar_tensor_tensor(out[:, 0:S - 1], bank[:, 1:S], c.vecs[:, w + 2:w + 3], out[:, 0:S - 1],
                                   ALU.mult, ALU.add).then_inc(c.emptied("dve", name, t), 1)
        v.drain()
        v.wait_ge(c.sem("gate_silu"), t + 1)
        v.tensor_tensor(act[:, t, :], tmp[:, 2 * (t % 2), :], tmp[:, 2 * (t % 2) + 1, :], ALU.mult) \
            .then_inc(c.sem("act"), 1)
        for _ in range(MOD_TILES * (t + 1) // FT - MOD_TILES * t // FT):
            next(ada, None)
    for _ in ada:
        pass
    for t in range(DT):
        v.wait_ge(*c.finished("fd", t))
        bank = c.bank("fd", t)
        v.tensor_tensor(x[:, t, :], x[:, t, :], bank, ALU.add).then_inc(c.emptied("dve", "fd", t), 1)
    v.wait_ge(*c.put_away("ssf", 0))
    v.reciprocal(rstd, rstd)
    v.drain()
    rows_times_root(x, x, "norm_f_g", DT, "block1", rstd)


def first_pool(c, g):
    kT, kr = c.view(BIG_ + 4096, H1, S), c.view(C_ + 5 * S, S)
    g.wait_ge(c.sem("kr_turned"), 1)
    for h in range(H1):
        g.tensor_copy(kT[64:96, h, :], kr[64:96]).then_inc(c.sem("kr_spread"), 1)


HA, AD = 8, 128
CKV = 256
IH, ID = 8, 64
TOPK = 128
ATT_SCALE = AD ** -0.5
INDEX_SCALE = IH ** -0.5 * ID ** -0.5
DH = 8
NE, NG, EG, EF = 32, 4, 8, 512
SLOTS = 64
NB = 48
ALPHA = 2.0 ** 0.25
LN_EPS = 1e-5
SET_ASIDE = -1e30
FUTURE = -1e38
TAKEN = -3e38
C_QA = 0
C_CK = C_QA + HA * AD
C_QI = C_CK + CKV
C_KI = C_QI + IH * ID
C_WI = C_KI + ID
C_DN = C_WI + IH
C_A = C_DN + 3 * D
C_B = C_A + DH
C_Z = C_B + DH
C_G = C_Z + D
LEVELS = (2, 4, 8, 16, 32, 64)


def plan_second(p):
    w = "w_in_2"
    p.job("ki", 0, "act", column_blocks(w, D, ("pair", C_KI, C_KI)))
    for t in range(4):
        p.job("qi", t, "act", column_blocks(w, D, span(C_QI + t * P)))
    p.align(8)
    small = p.weights(column_blocks(w, D, ("small",)))
    for t in range(TT):
        p.job("sm", t, "act", shared=(small, 8))
    for t in range(2):
        p.job("ck", t, "act", column_blocks(w, D, span(C_CK + t * P)))
    p.job("ssck", 0, "act")
    for i in range(3 * IH):
        p.job("is", i, "act")
    for h in range(HA):
        p.job("qa", h, "act", column_blocks(w, D, span(C_QA + h * P)))
    for h in range(HA):
        p.job("kh", h, "act", [("w_uk_2", h * 2 + k, ("head",)) for k in range(2)])
    for f in range(2):
        p.align(8)
        v = p.weights([("w_uv_2", (4 * f + j) * 2 + k, ("head",)) for k in range(2) for j in range(4)])
        for t in range(TT):
            p.job("vh", f * TT + t, "act", shared=(v, 8))
    n = HA * TT
    for i in range(n + 2):
        if i < n:
            p.job("s2", i, "dve")
        if 1 <= i <= n:
            p.job("p2", i - 1, "act")
        if i >= 2:
            p.job("o2", i - 2, "dve")
            if (i - 2) % HA == HA - 1:
                for f in range(2):
                    p.job("y2", (i - 2) // HA * 2 + f, "act")
    for t in range(24):
        p.job("dc", t, "dve", column_blocks(w, D, span(C_DN + t * P)))
        if t >= 2 and t - 2 < 16:
            p.job("l2", t - 2, "act")
    p.job("G", 0, "act")
    for t in range(TT):
        for b in (2 * t, 2 * t + 1):
            p.job("kt", b, "dve")
            p.job("vt", b, "dve")
            p.job("gb", b, "act")
            p.job("kk", b, "dve")
            p.job("qk", b, "dve")
        for b in (2 * t, 2 * t + 1):
            p.job("la", b, "dve")
        for b in (2 * t, 2 * t + 1):
            p.job("lb", b, "act")
        for l in range(len(LEVELS)):
            for b in (2 * t, 2 * t + 1):
                p.job("P%d" % l, b, "dve")
            for b in (2 * t, 2 * t + 1):
                p.job("Y%d" % l, b, "act")
                if l < len(LEVELS) - 1:
                    p.job("X%d" % l, b, "dve")
        for b in (2 * t, 2 * t + 1):
            p.job("u", b, "act")
            p.job("w", b, "dve")
        for b in (2 * t, 2 * t + 1):
            p.job("ws", b, "dve")
        for b in (2 * t, 2 * t + 1):
            p.job("o", b, "act")
            p.job("st", b, "dve")
    for h in range(DH):
        p.job("sso", h, "act")
        p.job("z", h, "act", column_blocks(w, D, span(C_Z + h * P)))
    for t in range(DT):
        p.job("ga", t, "act", column_blocks(w, D, span(C_G + t * P)))
        p.job("ba", t, "dve", column_blocks("w_br_att_2", D, span(t * P)))
        p.job("gd", t, "act", column_blocks(w, D, span(C_G + D + t * P)))
        p.job("bd", t, "dve", column_blocks("w_br_dn_2", D, span(t * P)))
    for t in range(DT):
        p.job("wo2", t, "dve", column_blocks("w_out_2", D, span(t * P)))
    p.job("lmean", 0, "act")
    p.job("lvar", 0, "act")
    p.align(8)
    route = p.weights([("route", k, ("route",)) for k in range(DT)])
    for t in range(TT):
        p.job("rt", t, "act", shared=(route, 8))
    for i in range(2 * TT):
        p.job("ht", i, "act")
    for t in range(TT):
        p.job("rank", t, "act")
    p.job("total", 0, "act")
    for i in range(2 * TT):
        p.job("xt", i, "dve")


B0 = 8192
QI_, KI_, CK_, MADD_ = B0, B0 + 2048, B0 + 2560, B0 + 3584
QA_, KH_, VH_ = B0 + 5632, B0 + 9728, B0 + 13824
Y_, YT_, PB_ = B0 + 17920, B0 + 19968, B0 + 24064
RS2_ = PB_ + 2048
Q_, K_, V_, BA_ = B0, B0 + 4096, B0 + 8192, B0 + 12288
QE_, ST_, MSK_ = BA_ + 8192, BA_ + 9216, BA_ + 10240
(WI_S, ARAW_S, G_S, BETA_S, CUM_S, LAST_S, EG_S, ET_S, EL_S, KB_S, NALOG_S, DTB_S, TMP_S, TMP2_S) = \
    (32 * i for i in range(14))
M8_S, NM_S, RSUM_S, RINV_S = 448, 472, 476, 480
SMALL = 576


def tokens(small, at):
    return small[:, at:at + 32].rearrange("p (t h) -> p t h", t=TT)


def sums(c, pe, name, tiles, source, counted, squares, used=True):
    pe.wait_ge(*c.bank_free(name[0], name[1]))
    bank = c.bank(name[0], name[1])
    for k in range(tiles):
        squares[0] += 1
        pe.wait_ge(c.sem(counted), squares[0])
        m = pe.matmul(bank, c.ones[:, :], source(k), start=k == 0, stop=k == tiles - 1)
        m.then_inc(c.sem("job_done") if k == tiles - 1 else c.sem("squares2_used"), 1)


def second_pe(c, pe):
    x, h = c.view(X_, DT, S), c.view(H_, DT, S)
    qi, ki, ck = c.view(QI_, 4, S), c.view(KI_, S), c.view(CK_, 2, S)
    qa, kh, vh = c.view(QA_, HA, S), c.view(KH_, HA, S), c.view(VH_, TT, D)
    y, prob, probT = c.view(Y_, 2, D), c.view(PB_, 2, S), c.view(PB_ + 1024, 2, TT, P)
    sq = c.view(Y_, 4, S)
    sqb = c.view(BA_, 4, S)
    done = c.sem("job_done")
    squares = [0]

    def gemm(name, i, rhs, tiles):
        if c.reused(name, i):
            pe.wait_ge(*c.bank_free(name, i))
        bank, at = c.bank(name, i), c.plan.first[name, i]
        for k in range(tiles):
            if k == 0 or (at + k) % CHUNK == 0:
                pe.wait_ge(*c.landed(at + k))
            m = pe.matmul(bank, c.weight(at + k), rhs(k), start=k == 0, stop=k == tiles - 1)
        m.then_inc(c.sem("job_done"), 1)

    pe.wait_ge(c.sem("constants"), 2)
    pe.wait_ge(c.sem("h"), DT)
    gemm("ki", 0, lambda k: h[:, k, :], DT)
    for t in range(4):
        gemm("qi", t, lambda k: h[:, k, :], DT)
    for t in range(TT):
        pe.wait_ge(*c.bank_free("sm", t))
        bank = c.bank("sm", t)
        pe.wait_ge(*c.landed(c.plan.first["sm", t]))
        for k in range(DT):
            m = pe.matmul(bank[:, 0:24], h[:, k, t * P:(t + 1) * P],
                          c.weight(c.plan.first["sm", t] + k)[:, 0:24], start=k == 0, stop=k == DT - 1)
        m.then_inc(done, 1)
    for t in range(2):
        gemm("ck", t, lambda k: h[:, k, :], DT)
    sums(c, pe, ("ssck", 0), 2, lambda k: sq[:, k, :], "squares2", squares)
    pe.wait_ge(*c.put_away("ki", 0))
    for i in range(3 * IH):
        t, hd = 1 + i // IH, i % IH
        r = 64 * (hd % 2)
        pe.wait_ge(*c.bank_free("is", i))
        bank = c.bank("is", i)
        pe.wait_ge(*c.put_away("qi", hd // 2))
        pe.matmul(bank[:, 0:(t + 1) * P], qi[r:r + 64, hd // 2, t * P:(t + 1) * P], ki[r:r + 64, 0:(t + 1) * P],
                  start=True, stop=True).then_inc(done, 1)
    for i in range(HA):
        gemm("qa", i, lambda k: h[:, k, :], DT)
    pe.wait_ge(c.sem("ckn"), 2)
    for i in range(HA):
        gemm("kh", i, lambda k: ck[:, k, :], 2)
    for i in range(2 * TT):
        f, t = i // TT, i % TT
        pe.wait_ge(*c.bank_free("vh", i))
        bank = c.bank("vh", i)
        pe.wait_ge(*c.landed(c.plan.first["vh", i]))
        for k in range(2):
            m = pe.matmul(bank, ck[:, k, t * P:(t + 1) * P], c.weight(c.plan.first["vh", i] + 4 * k, 4),
                          start=k == 0, stop=k == 1)
        m.then_inc(done, 1)
    n = HA * TT
    for i in range(n + 2):
        if i < n:
            t, hd = i // HA, i % HA
            pe.wait_ge(*c.bank_free("s2", i))
            bank = c.bank("s2", i)
            pe.wait_ge(*c.put_away("qa", hd))
            pe.wait_ge(*c.put_away("kh", hd))
            pe.matmul(bank[:, 0:(t + 1) * P], qa[:, hd, t * P:(t + 1) * P], kh[:, hd, 0:(t + 1) * P],
                      start=True, stop=True).then_inc(done, 1)
        if 1 <= i <= n:
            j = i - 1
            pe.wait_ge(*c.bank_free("p2", j))
            bank = c.bank("p2", j)
            pe.wait_ge(c.sem("prob2"), j + 1)
            for k in range(j // HA + 1):
                m = pe.transpose(bank[:, k * P:(k + 1) * P], prob[:, j % 2, k * P:(k + 1) * P], c.ident[:, :])
            m.then_inc(done, 1)
        if i >= 2:
            j = i - 2
            t, hd = j // HA, j % HA
            pe.wait_ge(*c.bank_free("o2", j))
            bank = c.bank("o2", j)
            pe.wait_ge(*c.put_away("p2", j))
            pe.wait_ge(*c.put_away("vh", 2 * TT - 1))
            for k in range(t + 1):
                m = pe.matmul(bank[:, 0:AD], probT[:, j % 2, k, :], vh[:, k, hd * P:(hd + 1) * P],
                              start=k == 0, stop=k == t)
            m.then_inc(done, 1)
            if hd == HA - 1:
                for f in range(2):
                    pe.wait_ge(*c.bank_free("y2", 2 * t + f))
                    bank = c.bank("y2", 2 * t + f)
                    pe.wait_ge(*c.put_away("o2", j))
                    for g in range(4):
                        m = pe.transpose(bank[:, g * P:(g + 1) * P], y[:, t % 2, (4 * f + g) * P:(4 * f + g + 1) * P],
                                         c.ident[:, :])
                    m.then_inc(done, 1)
    for t in range(24):
        gemm("dc", t, lambda k: h[:, k, :], DT)
        if 2 <= t < 18:
            sums(c, pe, ("l2", t - 2), 1, lambda k: sqb[:, (t - 2) % 4, :], "squares2", squares)
    pe.wait_ge(c.sem("masks"), 1)
    tri = c.view(MSK_, 9, P)[:, 7, :]
    g = tokens(c.small, G_S)
    pe.wait_ge(*c.bank_free("G", 0))
    bank = c.bank("G", 0)
    pe.wait_ge(c.sem("g"), 1)
    for t in range(TT):
        pe.matmul(bank[:, 8 * t:8 * t + 8], tri, g[:, t, :], start=True, stop=True)
        m = pe.matmul(bank[:, 32 + 8 * t:40 + 8 * t], c.ones[:, :], g[:, t, :], start=True, stop=True)
    m.then_inc(done, 1)
    q, k_, v_ = c.view(Q_, DH, S), c.view(K_, DH, S), c.view(V_, DH, S)
    st = c.view(ST_, DH, P)

    def arr(b, i):
        return c.view(BA_ + (b % 2) * 4096 + 512 * i, 4, P)

    def heads(b):
        return range(4 * (b % 2), 4 * (b % 2) + 4)

    def each(name, b, f):
        pe.wait_ge(*c.bank_free(name, b))
        bank = c.bank(name, b)
        for j, hd in enumerate(heads(b)):
            m = f(bank[:, j * P:(j + 1) * P], j, hd)
        m.then_inc(done, 1)

    def mm(out, lhsT, rhs, start=True, stop=True):
        return pe.matmul(out, lhsT, rhs, start=start, stop=stop)

    for t in range(TT):
        ts = slice(t * P, (t + 1) * P)
        pair = (2 * t, 2 * t + 1)
        for b in pair:
            pe.wait_ge(c.sem("k_norm"), 4 * (b % 2) + 4)
            each("kt", b, lambda o, j, hd: pe.transpose(o, k_[:, hd, ts], c.ident[:, :]))
            pe.wait_ge(c.sem("v_silu"), 4 * (b % 2) + 4)
            each("vt", b, lambda o, j, hd: pe.transpose(o, v_[:, hd, ts], c.ident[:, :]))
            each("gb", b, lambda o, j, hd: mm(o, g[:, t, hd:hd + 1].to_broadcast([P, P]), tri))
            each("kk", b, lambda o, j, hd: mm(o, k_[:, hd, ts], k_[:, hd, ts]))
            pe.wait_ge(c.sem("q_norm"), 4 * (b % 2) + 4)
            each("qk", b, lambda o, j, hd: mm(o, k_[:, hd, ts], q[:, hd, ts]))
        for b in pair:
            pe.wait_ge(c.sem("unit"), b + 1)
            each("la", b, lambda o, j, hd: pe.transpose(o, arr(b, 3)[:, j, :], c.ident[:, :]))
        for b in pair:
            pe.wait_ge(*c.put_away("la", b))
            each("lb", b, lambda o, j, hd: pe.transpose(o, arr(b, 6)[:, j, :], c.ident[:, :]))
        for l in range(len(LEVELS)):
            last = l == len(LEVELS) - 1
            for b in pair:
                pe.wait_ge(*c.put_away("Y%d" % (l - 1) if l else "la", b))
                each("P%d" % l, b, lambda o, j, hd: mm(o, arr(b, 3)[:, j, :], arr(b, 6)[:, j, :]))
            for b in pair:
                pe.wait_ge(*c.put_away("P%d" % l, b))
                pe.wait_ge(*c.put_away("X%d" % (l - 1) if l else "lb", b))
                each("Y%d" % l, b, lambda o, j, hd: mm(o, arr(b, 5)[:, j, :], arr(b, 7)[:, j, :]))
                if not last:
                    each("X%d" % l, b, lambda o, j, hd: mm(o, arr(b, 7)[:, j, :], arr(b, 5)[:, j, :]))
        for b in pair:
            pe.wait_ge(*c.put_away("Y%d" % (len(LEVELS) - 1), b))
            pe.wait_ge(*c.put_away("vt", b))
            each("u", b, lambda o, j, hd: mm(o, arr(b, 6)[:, j, :], arr(b, 2)[:, j, :]))
            each("w", b, lambda o, j, hd: mm(o, arr(b, 0)[:, j, :], arr(b, 6)[:, j, :]))
        for b in pair:
            pe.wait_ge(*c.put_away("w", b))
            if t:
                pe.wait_ge(*c.put_away("st", b - 2))
            else:
                pe.wait_ge(c.sem("state0"), 1)
            each("ws", b, lambda o, j, hd: mm(o, arr(b, 7)[:, j, :], st[:, hd, :]))
        for b in pair:
            pe.wait_ge(*c.put_away("ws", b))
            pe.wait_ge(c.sem("q_decayed"), b + 1)

            def out(o, j, hd):
                mm(o, st[:, hd, :], q[:, hd, ts], stop=False)
                return mm(o, arr(b, 5)[:, j, :], arr(b, 4)[:, j, :], start=False)
            each("o", b, out)
            each("st", b, lambda o, j, hd: mm(o, arr(b, 1)[:, j, :], arr(b, 5)[:, j, :]))
    for hd in range(DH):
        sums(c, pe, ("sso", hd), 1, lambda k: sqb[:, hd % 4, :], "squares2", squares)
        gemm("z", hd, lambda k: h[:, k, :], DT)
    yT, mg = c.view(K_, DT, S), c.view(V_, DT, S)
    pe.wait_ge(c.sem("y_back"), 16)
    for t in range(DT):
        gemm("ga", t, lambda k: h[:, k, :], DT)
        gemm("ba", t, lambda k: yT[:, k, :], DT)
        gemm("gd", t, lambda k: h[:, k, :], DT)
        pe.wait_ge(c.sem("y_dn"), DT)
        gemm("bd", t, lambda k: q[:, k, :], DT)
    pe.wait_ge(*c.put_away("bd", DT - 1))
    for t in range(DT):
        gemm("wo2", t, lambda k: mg[:, k, :], DT)
    pe.wait_ge(*c.bank_free("lmean", 0))
    bank = c.bank("lmean", 0)
    for k in range(DT):
        pe.wait_ge(*c.put_away("wo2", k))
        m = pe.matmul(bank, c.ones[:, :], x[:, k, :], start=k == 0, stop=k == DT - 1)
    m.then_inc(done, 1)
    sums(c, pe, ("lvar", 0), DT, lambda k: sqb[:, k % 4, :], "squares2", squares)
    pe.wait_ge(c.sem("h3"), DT)
    for t in range(TT):
        pe.wait_ge(*c.bank_free("rt", t))
        bank = c.bank("rt", t)
        pe.wait_ge(*c.landed(c.plan.first["rt", t]))
        for k in range(DT):
            m = pe.matmul(bank[:, 0:36], h[:, k, t * P:(t + 1) * P],
                          c.weight(c.plan.first["rt", t] + k)[:, 0:36], start=k == 0, stop=k == DT - 1)
        m.then_inc(done, 1)
    for i in range(2 * TT):
        t, f = i // 2, i % 2
        pe.wait_ge(*c.bank_free("ht", i))
        bank = c.bank("ht", i)
        for g_ in range(4):
            m = pe.transpose(bank[:, g_ * P:(g_ + 1) * P], h[:, 4 * f + g_, t * P:(t + 1) * P], c.ident[:, :])
        m.then_inc(done, 1)
    tris = c.view(MSK_, 9, P)[:, 8, :]
    sel = c.route[:, RT_SEL:RT_SEL + 128].rearrange("p (t e) -> p t e", t=TT)
    pe.wait_ge(c.sem("chosen"), 1)
    for t in range(TT):
        pe.wait_ge(*c.bank_free("rank", t))
        bank = c.bank("rank", t)
        m = pe.matmul(bank[:, 0:NE], tris, sel[:, t, :], start=True, stop=t == 0)
        for s in range(t):
            m = pe.matmul(bank[:, 0:NE], c.ones[:, :], sel[:, s, :], start=False, stop=s == t - 1)
        m.then_inc(done, 1)
    pe.wait_ge(*c.bank_free("total", 0))
    bank = c.bank("total", 0)
    for t in range(TT):
        m = pe.matmul(bank[:, 0:NE], c.ones[:, :], sel[:, t, :], start=t == 0, stop=t == TT - 1)
    m.then_inc(done, 1)
    for i in range(2 * TT):
        t, f = i // 2, i % 2
        pe.wait_ge(*c.bank_free("xt", i))
        bank = c.bank("xt", i)
        for g_ in range(4):
            m = pe.transpose(bank[:, g_ * P:(g_ + 1) * P], x[:, 4 * f + g_, t * P:(t + 1) * P], c.ident[:, :])
        m.then_inc(done, 1)


def second_act(c, a):
    x, h = c.view(X_, DT, S), c.view(H_, DT, S)
    qi, ki, ck = c.view(QI_, 4, S), c.view(KI_, S), c.view(CK_, 2, S)
    qa, kh, vh = c.view(QA_, HA, S), c.view(KH_, HA, S), c.view(VH_, TT, D)
    y, yT, prob, probT = c.view(Y_, 2, D), c.view(YT_, DT, S), c.view(PB_, 2, S), c.view(PB_ + 1024, 2, S)
    sq, sqb, relu = c.view(Y_, 4, S), c.view(BA_, 4, S), c.view(PB_, 4, S)
    rstd = c.view(RS2_, S)
    sm = c.small
    sem = c.sem

    def put(name, i, out, func=ACT.Copy, cols=512, **kw):
        a.wait_ge(*c.finished(name, i))
        bank = c.bank(name, i)
        a.activation(out, bank[:, 0:cols], func, **kw).then_inc(c.emptied("act", name, i), 1)

    a.wait_ge(c.sem("vectors"), 16)
    a.wait_ge(c.sem("constants"), 2)
    put("ki", 0, ki)
    for t in range(4):
        put("qi", t, qi[:, t, :])
    for t in range(TT):
        a.wait_ge(*c.finished("sm", t))
        bank = c.bank("sm", t)
        a.activation(tokens(sm, WI_S)[:, t, :], bank[:, 0:8], ACT.Copy, scale=INDEX_SCALE)
        a.activation(tokens(sm, ARAW_S)[:, t, :], bank[:, 8:16], ACT.Copy)
        a.activation(tokens(sm, BETA_S)[:, t, :], bank[:, 16:24], ACT.Sigmoid).then_inc(c.emptied("act", "sm", t), 1)
    for t in range(2):
        a.wait_ge(*c.finished("ck", t))
        bank = c.bank("ck", t)
        a.activation(sq[:, t, :], bank, ACT.Square).then_inc(sem("squares2"), 1)
        a.activation(ck[:, t, :], bank, ACT.Copy).then_inc(c.emptied("act", "ck", t), 1)
    put("ssck", 0, rstd, ACT.Sqrt, bias=c.cons[:, 0:1], scale=1.0 / CKV)
    for i in range(3 * IH):
        w = (2 + i // IH) * P
        if i >= 4:
            a.wait_ge(c.sem("is_added"), i - 3)
        put("is", i, relu[:, i % 4, 0:w], ACT.Relu, w)
    for i in range(HA):
        put("qa", i, qa[:, i, :])
    for i in range(HA):
        put("kh", i, kh[:, i, :])
    for i in range(2 * TT):
        put("vh", i, vh[:, i % TT, 512 * (i // TT):512 * (i // TT) + 512])
    araw, tmp, tmp2 = sm[:, ARAW_S:ARAW_S + 32], sm[:, TMP_S:TMP_S + 32], sm[:, TMP2_S:TMP2_S + 32]
    a.wait_ge(c.sem("a_abs"), 1)
    a.activation(tmp, tmp, ACT.Exp, scale=-1.0)
    a.drain()
    a.activation(tmp, tmp, ACT.Ln, bias=1.0)
    nal = sm[:, NALOG_S:NALOG_S + 32]
    a.activation(nal, nal, ACT.Exp).then_inc(sem("a_soft"), 1)
    n = HA * TT
    for i in range(n + 2):
        if i < n:
            w = (i // HA + 1) * P
            a.wait_ge(c.sem("nmax2"), i + 1)
            a.activation(prob[:, i % 2, 0:w], prob[:, i % 2, 0:w], ACT.Exp, bias=sm[:, NM_S + i % 4:NM_S + i % 4 + 1],
                         accum_out=sm[:, RSUM_S + i % 4:RSUM_S + i % 4 + 1]).then_inc(sem("prob2"), 1)
        if 1 <= i <= n:
            j = i - 1
            w = (j // HA + 1) * P
            if j >= 2:
                a.wait_ge(*c.finished("o2", j - 2))
            put("p2", j, probT[:, j % 2, 0:w], cols=w)
        if i >= 2 and (i - 2) % HA == HA - 1:
            t = (i - 2) // HA
            for f in range(2):
                a.wait_ge(*c.finished("y2", 2 * t + f))
                bank = c.bank("y2", 2 * t + f)
                a.activation(yT[:, 4 * f:4 * f + 4, t * P:(t + 1) * P], bank.rearrange("p (j q) -> p j q", j=4),
                             ACT.Copy).then_inc(c.emptied("act", "y2", 2 * t + f), 1)
    qkv = c.view(Q_, 24, S)
    a.wait_ge(*c.put_away("o2", n - 1))
    for t in range(24):
        a.wait_ge(*c.finished("dc", t))
        bank = c.bank("dc", t)
        w = VECS["conv_w_2"][0] + 4 * t
        a.activation(qkv[:, t, :], bank, ACT.Copy, scale=c.vecs[:, w + 3:w + 4]).then_inc(sem("last_tap"), 1)
        a.wait_ge(*c.put_away("dc", t))
        m = a.activation(qkv[:, t, :], qkv[:, t, :], ACT.Silu)
        if t < 16:
            a.drain()
            if t >= 4:
                a.wait_ge(*c.finished("l2", t - 4))
            a.activation(sqb[:, t % 4, :], qkv[:, t, :], ACT.Square).then_inc(sem("squares2"), 1)
        else:
            m.then_inc(sem("v_silu"), 1)
        if 2 <= t < 18:
            if t >= 3:
                a.wait_ge(c.sem("l2_used"), t - 2)
            put("l2", t - 2, rstd, ACT.Sqrt, bias=c.cons[:, 0:1])
    a.wait_ge(*c.finished("G", 0))
    bank = c.bank("G", 0)
    a.activation(sm[:, CUM_S:CUM_S + 64], bank[:, 0:64], ACT.Copy).then_inc(c.emptied("act", "G", 0), 1)
    a.drain()
    a.activation(sm[:, EG_S:EG_S + 32], sm[:, CUM_S:CUM_S + 32], ACT.Exp)
    a.activation(sm[:, EL_S:EL_S + 32], sm[:, LAST_S:LAST_S + 32], ACT.Exp)
    a.wait_ge(c.sem("g_tail"), 1)
    a.activation(sm[:, ET_S:ET_S + 32], sm[:, ET_S:ET_S + 32], ACT.Exp).then_inc(sem("g_exps"), 1)

    def arr(b, i):
        return c.view(BA_ + (b % 2) * 4096 + 512 * i, S)

    q = c.view(Q_, DH, S)
    for t in range(TT):
        pair = (2 * t, 2 * t + 1)
        for b in pair:
            a.wait_ge(c.sem("decays"), b + 1)
            put("gb", b, c.view(QE_ + 512 * (b % 2), S), ACT.Exp)
            a.activation(arr(b, 7), arr(b, 7), ACT.Exp)
            a.activation(arr(b, 5), arr(b, 5), ACT.Exp, scale=-1.0).then_inc(sem("decay_exps"), 1)
        for b in pair:
            put("lb", b, arr(b, 5))
        for l in range(len(LEVELS)):
            for b in pair:
                put("Y%d" % l, b, arr(b, 6))
        for b in pair:
            put("u", b, arr(b, 3))
        for b in pair:
            a.wait_ge(*c.finished("o", b))
            bank = c.bank("o", b)
            g0 = 4 * (b % 2)
            a.activation(q[:, g0:g0 + 4, t * P:(t + 1) * P], bank.rearrange("p (j q) -> p j q", j=4), ACT.Copy) \
                .then_inc(c.emptied("act", "o", b), 1)
    rs, zt = c.view(BA_ + 2048, 2, S), c.view(BA_ + 3072, 2, S)
    a.wait_ge(*c.put_away("st", 7))
    a.wait_ge(*c.put_away("o", 7))
    for hd in range(DH):
        if hd >= 4:
            a.wait_ge(*c.finished("sso", hd - 4))
        a.activation(sqb[:, hd % 4, :], q[:, hd, :], ACT.Square).then_inc(sem("squares2"), 1)
        if hd >= 2:
            a.wait_ge(c.sem("y_dn"), hd - 1)
        put("sso", hd, rs[:, hd % 2, :], ACT.Sqrt, bias=c.cons[:, 0:1], scale=1.0 / P)
        put("z", hd, zt[:, hd % 2, :], ACT.Silu)
    gate = c.view(BA_ + 4096, 4, S)
    for t in range(DT):
        if t >= 2:
            a.wait_ge(*c.put_away("ba", t - 2))
        put("ga", t, gate[:, t % 2, :], ACT.Sigmoid)
        if t >= 2:
            a.wait_ge(*c.put_away("bd", t - 2))
        put("gd", t, gate[:, 2 + t % 2, :], ACT.Sigmoid)
    mean, rs = c.view(BA_ + 2048, S), c.view(BA_ + 2560, S)
    put("lmean", 0, mean, ACT.Copy, scale=1.0 / D)
    for k in range(DT):
        a.wait_ge(c.sem("centred2"), k + 1)
        if k >= 4:
            a.wait_ge(c.sem("squares2_used"), 1 + k - 3)
        a.activation(sqb[:, k % 4, :], x[:, k, :], ACT.Square).then_inc(sem("squares2"), 1)
    put("lvar", 0, rs, ACT.Sqrt, bias=c.cons[:, 1:2], scale=1.0 / D)
    logits = c.route[:, RT_LG:RT_LG + 144].rearrange("p (t e) -> p t e", t=TT)
    for t in range(TT):
        put("rt", t, logits[:, t, :], cols=36)
    htok = c.view(HTOK_, TT, D)
    for i in range(2 * TT):
        put("ht", i, htok[:, i // 2, 512 * (i % 2):512 * (i % 2) + 512])
    a.wait_ge(c.sem("route_exp"), 1)
    ex = c.route[:, RT_EXP:RT_EXP + 20]
    a.activation(ex, ex, ACT.Exp).then_inc(sem("route_exps"), 1)
    for t in range(TT):
        put("rank", t, c.route[:, RT_RANK + 32 * t:RT_RANK + 32 * t + 32], cols=NE)
    put("total", 0, c.route[:, RT_TOT:RT_TOT + 32], cols=NE)


def second_dve(c, v):
    x, h = c.view(X_, DT, S), c.view(H_, DT, S)
    ck, madd = c.view(CK_, 2, S), c.view(MADD_, TT, S)
    y, prob = c.view(Y_, 2, D), c.view(PB_, 2, S)
    relu, score, work = c.view(PB_, 4, S), c.view(YT_, 3, S), c.view(YT_ + 1536, 3, S)
    rstd = c.view(RS2_, S)
    sm, sem = c.small, c.sem
    v.wait_ge(c.sem("mod"), 1)
    for k in range(DT):
        v.tensor_scalar(h[:, k, :], x[:, k, :], c.mod[:, 8 + k:9 + k], c.mod[:, k:k + 1], ALU.mult, ALU.add) \
            .then_inc(sem("h"), 1)
    v.wait_ge(*c.put_away("sm", TT - 1))
    v.wait_ge(c.sem("decay_params"), 32)
    araw, tmp, tmp2 = sm[:, ARAW_S:ARAW_S + 32], sm[:, TMP_S:TMP_S + 32], sm[:, TMP2_S:TMP2_S + 32]
    v.tensor_tensor(araw, araw, sm[:, DTB_S:DTB_S + 32], ALU.add)
    v.drain()
    v.tensor_scalar(tmp, araw, -1.0, None, ALU.mult)
    v.drain()
    v.tensor_tensor(tmp, tmp, araw, ALU.max).then_inc(sem("a_abs"), 1)
    v.tensor_scalar(tmp2, araw, 0.0, None, ALU.max)
    v.wait_ge(*c.put_away("ssck", 0))
    v.reciprocal(rstd, rstd)
    v.drain()
    for k in range(2):
        v.scalar_tensor_tensor(ck[:, k, :], ck[:, k, :], c.vec("kv_norm_g_2", k), rstd, ALU.mult, ALU.mult) \
            .then_inc(sem("ckn"), 1)
    wi = tokens(sm, WI_S)
    v.wait_ge(*c.put_away("sm", TT - 1))
    for i in range(3 * IH):
        t, hd = 1 + i // IH, i % IH
        w = (t + 1) * P
        v.wait_ge(*c.put_away("is", i))
        if hd == 0:
            v.tensor_scalar(score[:, t - 1, 0:w], relu[:, i % 4, 0:w], wi[:, t, 0:1], None, ALU.mult) \
                .then_inc(sem("is_added"), 1)
        else:
            v.scalar_tensor_tensor(score[:, t - 1, 0:w], relu[:, i % 4, 0:w], wi[:, t, hd:hd + 1],
                                   score[:, t - 1, 0:w], ALU.mult, ALU.add).then_inc(sem("is_added"), 1)
        v.drain()
    m8 = sm[:, M8_S:M8_S + 24].rearrange("p (t e) -> p t e", t=3)
    v.wait_ge(c.sem("causal"), 3)
    for t in range(3):
        v.tensor_copy(work[:, t, 0:(t + 2) * P], score[:, t, 0:(t + 2) * P])
    v.drain()
    for _ in range(TOPK // 8):
        for t in range(3):
            v.max(m8[:, t, :], work[:, t, 0:(t + 2) * P])
        v.drain()
        for t in range(3):
            v.match_replace(work[:, t, 0:(t + 2) * P], m8[:, t, :], work[:, t, 0:(t + 2) * P], TAKEN)
        v.drain()
    for t in range(3):
        w = (t + 2) * P
        v.tensor_tensor(madd[:, t + 1, 0:w], work[:, t, 0:w], score[:, t, 0:w], ALU.is_equal)
    v.drain()
    for t in range(3):
        w = (t + 2) * P
        v.tensor_scalar(madd[:, t + 1, 0:w], madd[:, t + 1, 0:w], SET_ASIDE, None, ALU.mult)
    v.drain()
    v.wait_ge(c.sem("a_soft"), 1)
    v.tensor_tensor(tmp, tmp, tmp2, ALU.add)
    v.drain()
    v.scalar_tensor_tensor(sm[:, G_S:G_S + 32], tmp, -1.0, sm[:, NALOG_S:NALOG_S + 32], ALU.mult, ALU.mult) \
        .then_inc(sem("g"), 1)
    n = HA * TT
    v.wait_ge(c.sem("causal"), 4)
    for i in range(n + 2):
        if i < n:
            t = i // HA
            w = (t + 1) * P
            v.wait_ge(*c.finished("s2", i))
            bank = c.bank("s2", i)
            if i >= 2:
                v.wait_ge(*c.finished("p2", i - 2))
            v.scalar_tensor_tensor(prob[:, i % 2, 0:w], bank[:, 0:w], ATT_SCALE, madd[:, t, 0:w], ALU.mult, ALU.add) \
                .then_inc(c.emptied("dve", "s2", i), 1)
            v.drain()
            v.tensor_reduce(sm[:, NM_S + i % 4:NM_S + i % 4 + 1], prob[:, i % 2, 0:w], AX.X, ALU.max, negate=True) \
                .then_inc(sem("nmax2"), 1)
        if i >= 2:
            j = i - 2
            t, hd = j // HA, j % HA
            v.wait_ge(c.sem("prob2"), j + 1)
            rinv = sm[:, RINV_S + j % 4:RINV_S + j % 4 + 1]
            v.reciprocal(rinv, sm[:, RSUM_S + j % 4:RSUM_S + j % 4 + 1])
            v.drain()
            v.wait_ge(*c.finished("o2", j))
            bank = c.bank("o2", j)
            if hd == 0 and t >= 2:
                v.wait_ge(*c.put_away("y2", 2 * (t - 2) + 1))
            v.tensor_scalar(y[:, t % 2, hd * P:(hd + 1) * P], bank[:, 0:AD], rinv, None, ALU.mult) \
                .then_inc(c.emptied("dve", "o2", j), 1)
    qkv = c.view(Q_, 24, S)

    def norm(t):
        v.wait_ge(*c.put_away("l2", t))
        v.reciprocal(rstd, rstd)
        v.drain()
        scale = P ** -0.5 if t < 8 else 1.0
        v.scalar_tensor_tensor(qkv[:, t, :], qkv[:, t, :], scale, rstd, ALU.mult, ALU.mult) \
            .then_inc(sem("q_norm" if t < 8 else "k_norm"), 1)
        v.drain()
        v.memset(sm[:, TMP2_S:TMP2_S + 1], 0.0).then_inc(sem("l2_used"), 1)

    for t in range(24):
        v.wait_ge(*c.finished("dc", t))
        bank = c.bank("dc", t)
        v.wait_ge(c.sem("last_tap"), t + 1)
        w = VECS["conv_w_2"][0] + 4 * t
        for s in (1, 2, 3):
            m = v.scalar_tensor_tensor(qkv[:, t, s:S], bank[:, 0:S - s], c.vecs[:, w + 3 - s:w + 4 - s],
                                       qkv[:, t, s:S], ALU.mult, ALU.add)
            if s < 3:
                v.drain()
        m.then_inc(c.emptied("dve", "dc", t), 1)
        if 2 <= t < 18:
            norm(t - 2)
    v.wait_ge(*c.put_away("G", 0))
    cum, last = sm[:, CUM_S:CUM_S + 32], sm[:, LAST_S:LAST_S + 32]
    v.tensor_tensor(sm[:, ET_S:ET_S + 32], last, cum, ALU.subtract).then_inc(sem("g_tail"), 1)
    v.wait_ge(c.sem("g_exps"), 1)
    v.tensor_tensor(sm[:, KB_S:KB_S + 32], sm[:, BETA_S:BETA_S + 32], sm[:, EG_S:EG_S + 32], ALU.mult)
    v.drain()

    def arr(b, i):
        return c.view(BA_ + (b % 2) * 4096 + 512 * i, 4, P)

    def per_head(table, t, b):
        g0 = 4 * (b % 2)
        return tokens(sm, table)[:, t, g0:g0 + 4].unsqueeze(2).to_broadcast([P, 4, P])

    def wide(bank):
        return bank.rearrange("p (j q) -> p j q", j=4)

    q = c.view(Q_, DH, S)
    st = c.view(ST_, DH, P)
    masks = c.view(MSK_, 9, P)
    v.wait_ge(c.sem("masks"), 1)
    v.memset(c.view(ST_, DH * P), 0.0).then_inc(sem("state0"), 1)

    def mask(i):
        return masks[:, i, :].unsqueeze(1).to_broadcast([P, 4, P])

    for t in range(TT):
        pair = (2 * t, 2 * t + 1)
        for b in pair:
            g0 = 4 * (b % 2)
            if t:
                v.wait_ge(*c.finished("st", b - 2))
            v.wait_ge(*c.finished("kt", b))
            bank = c.bank("kt", b)
            v.tensor_tensor(arr(b, 0), wide(bank), per_head(KB_S, t, b), ALU.mult)
            v.tensor_tensor(arr(b, 1), wide(bank), per_head(ET_S, t, b), ALU.mult).then_inc(c.emptied("dve", "kt", b), 1)
            v.wait_ge(*c.finished("vt", b))
            bank = c.bank("vt", b)
            v.tensor_tensor(arr(b, 2), wide(bank), per_head(BETA_S, t, b), ALU.mult).then_inc(c.emptied("dve", "vt", b), 1)
            v.wait_ge(*c.finished("gb", b))
            bank = c.bank("gb", b)
            v.tensor_tensor(arr(b, 7), wide(bank), per_head(CUM_S, t, b), ALU.subtract)
            v.drain()
            v.tensor_scalar(arr(b, 5), arr(b, 7), 0.0, None, ALU.max)
            v.drain()
            v.tensor_scalar(arr(b, 7), arr(b, 7), 0.0, None, ALU.min).then_inc(sem("decays"), 1)
            v.wait_ge(c.sem("decay_masked"), 2 * b + 1)
            v.wait_ge(*c.finished("kk", b))
            bank = c.bank("kk", b)
            for j in range(4):
                beta = tokens(sm, BETA_S)[:, t, g0 + j:g0 + j + 1]
                m = v.scalar_tensor_tensor(arr(b, 3)[:, j, :], bank[:, j * P:(j + 1) * P], beta, arr(b, 5)[:, j, :],
                                           ALU.mult, ALU.mult)
            m.then_inc(c.emptied("dve", "kk", b), 1)
            v.drain()
            v.tensor_tensor(arr(b, 3), arr(b, 3), c.ident[:, :].unsqueeze(1).to_broadcast([P, 4, P]), ALU.add) \
                .then_inc(sem("unit"), 1)
            v.wait_ge(c.sem("decay_masked"), 2 * b + 2)
            v.wait_ge(*c.finished("qk", b))
            bank = c.bank("qk", b)
            v.tensor_tensor(arr(b, 4), wide(bank), arr(b, 7), ALU.mult).then_inc(c.emptied("dve", "qk", b), 1)
            v.wait_ge(*c.put_away("gb", b))
            qs = q[:, g0:g0 + 4, t * P:(t + 1) * P]
            v.tensor_tensor(qs, qs, c.view(QE_ + 512 * (b % 2), 4, P), ALU.mult).then_inc(sem("q_decayed"), 1)
        for b in pair:
            v.wait_ge(*c.finished("la", b))
            bank = c.bank("la", b)
            v.tensor_tensor(arr(b, 6), wide(bank), mask(0), ALU.mult).then_inc(c.emptied("dve", "la", b), 1)
        for l in range(len(LEVELS)):
            for b in pair:
                v.wait_ge(*c.finished("P%d" % l, b))
                bank = c.bank("P%d" % l, b)
                v.tensor_tensor(arr(b, 7), wide(bank), mask(l + 1), ALU.mult).then_inc(c.emptied("dve", "P%d" % l, b), 1)
            if l < len(LEVELS) - 1:
                for b in pair:
                    v.wait_ge(*c.finished("X%d" % l, b))
                    bank = c.bank("X%d" % l, b)
                    v.tensor_copy(arr(b, 5), wide(bank)).then_inc(c.emptied("dve", "X%d" % l, b), 1)
        for b in pair:
            v.wait_ge(*c.finished("w", b))
            bank = c.bank("w", b)
            v.tensor_copy(arr(b, 7), wide(bank)).then_inc(c.emptied("dve", "w", b), 1)
        for b in pair:
            v.wait_ge(*c.finished("ws", b))
            bank = c.bank("ws", b)
            v.wait_ge(*c.put_away("u", b))
            v.tensor_tensor(arr(b, 5), arr(b, 3), wide(bank), ALU.subtract).then_inc(c.emptied("dve", "ws", b), 1)
        for b in pair:
            v.wait_ge(*c.finished("st", b))
            bank = c.bank("st", b)
            g0 = 4 * (b % 2)
            for j in range(4):
                el = tokens(sm, EL_S)[:, t, g0 + j:g0 + j + 1]
                m = v.scalar_tensor_tensor(st[:, g0 + j, :], st[:, g0 + j, :], el, bank[:, j * P:(j + 1) * P],
                                           ALU.mult, ALU.add)
            m.then_inc(c.emptied("dve", "st", b), 1)
        v.drain()
    rs, zt = c.view(BA_ + 2048, 2, S), c.view(BA_ + 3072, 2, S)
    for hd in range(DH):
        v.wait_ge(*c.put_away("sso", hd))
        v.reciprocal(rs[:, hd % 2, :], rs[:, hd % 2, :])
        v.drain()
        v.scalar_tensor_tensor(q[:, hd, :], q[:, hd, :], c.vec("dn_norm_g_2"), rs[:, hd % 2, :], ALU.mult, ALU.mult)
        v.drain()
        v.wait_ge(*c.put_away("z", hd))
        v.tensor_tensor(q[:, hd, :], q[:, hd, :], zt[:, hd % 2, :], ALU.mult).then_inc(sem("y_dn"), 1)
    gate, mg, tmp = c.view(BA_ + 4096, 4, S), c.view(V_, DT, S), c.view(BA_ + 6144, S)
    for t in range(DT):
        v.wait_ge(*c.put_away("ga", t))
        v.wait_ge(*c.finished("ba", t))
        bank = c.bank("ba", t)
        v.tensor_tensor(mg[:, t, :], bank, gate[:, t % 2, :], ALU.mult).then_inc(c.emptied("dve", "ba", t), 1)
        v.wait_ge(*c.put_away("gd", t))
        v.wait_ge(*c.finished("bd", t))
        bank = c.bank("bd", t)
        v.tensor_tensor(tmp, bank, gate[:, 2 + t % 2, :], ALU.mult)
        v.drain()
        v.tensor_tensor(mg[:, t, :], mg[:, t, :], tmp, ALU.add).then_inc(c.emptied("dve", "bd", t), 1)
        v.drain()
    v.wait_ge(c.sem("x_scaled"), 1)
    for t in range(DT):
        v.wait_ge(*c.finished("wo2", t))
        bank = c.bank("wo2", t)
        v.scalar_tensor_tensor(x[:, t, :], bank, c.mod[:, 16 + t:17 + t], x[:, t, :], ALU.mult, ALU.add) \
            .then_inc(c.emptied("dve", "wo2", t), 1)
    mean, rs = c.view(BA_ + 2048, S), c.view(BA_ + 2560, S)
    v.wait_ge(*c.put_away("lmean", 0))
    for k in range(DT):
        v.tensor_tensor(x[:, k, :], x[:, k, :], mean, ALU.subtract).then_inc(sem("centred2"), 1)
    v.wait_ge(*c.put_away("lvar", 0))
    v.reciprocal(rs, rs)
    v.drain()
    for k in range(DT):
        v.scalar_tensor_tensor(x[:, k, :], x[:, k, :], c.vec("ln_g_2", k), rs, ALU.mult, ALU.mult)
    v.drain()
    for k in range(DT):
        v.tensor_scalar(x[:, k, :], x[:, k, :], c.vec("ln_b_2", k), None, ALU.add)
    v.drain()
    for k in range(DT):
        v.tensor_scalar(h[:, k, :], x[:, k, :], c.mod[:, 32 + k:33 + k], c.mod[:, 24 + k:25 + k], ALU.mult, ALU.add) \
            .then_inc(sem("h3"), 1)


def second_pool(c, g):
    g.wait_ge(c.sem("h"), DT)
    score, madd = c.view(YT_, 3, S), c.view(MADD_, TT, S)
    g.memset(madd[:, 0, 0:P], 0.0)
    g.memset(c.cons[:, 1:2], LN_EPS)
    for t in range(1, TT):
        g.wait_ge(c.sem("is_added"), IH * t)
        own = score[:, t - 1, t * P:(t + 1) * P]
        g.affine_select(out=own, in_=own, compare_op=ALU.is_ge, fill=FUTURE, base=0, pattern=[[-1, P]],
                        channel_multiplier=1).then_inc(c.sem("causal"), 1)
    g.drain()
    g.affine_select(out=madd[:, 0, 0:P], in_=madd[:, 0, 0:P], compare_op=ALU.is_ge, fill=SET_ASIDE, base=0,
                    pattern=[[-1, P]], channel_multiplier=1).then_inc(c.sem("causal"), 1)
    g.wait_ge(*c.put_away("y2", 2 * TT - 1))
    g.dma_start(c.y_spill, c.view(YT_, DT, S)).then_inc(c.sem("y_spilled"), 16)
    g.wait_ge(c.sem("y_spilled"), 16)
    masks = c.view(MSK_, 9, P)
    g.memset(c.view(MSK_, 7 * P), -1.0)
    g.memset(c.view(MSK_ + 7 * P, 2 * P), 1.0)
    g.drain()
    for i, b in enumerate((1,) + LEVELS):
        m = masks[:, i, :].rearrange("p (n h j) -> p n h j", h=2, j=b)
        n = P // (2 * b)
        g.affine_select(out=m, in_=m, compare_op=ALU.is_ge, fill=0.0, base=0,
                        pattern=[[-2 * b, n], [0, 2], [0, b]], channel_multiplier=1)
        g.drain()
        g.affine_select(out=m, in_=m, compare_op=ALU.is_ge, fill=0.0, base=b - 1,
                        pattern=[[2 * b, n], [0, 2], [0, b]], channel_multiplier=-1)
        g.drain()
        g.affine_select(out=m, in_=m, compare_op=ALU.is_gt, fill=0.0, base=0,
                        pattern=[[0, n], [1, 2], [0, b]], channel_multiplier=0)
        g.drain()
        g.affine_select(out=masks[:, i, :], in_=masks[:, i, :], compare_op=ALU.not_equal, fill=1.0, base=0,
                        pattern=[[-1, P]], channel_multiplier=1)
    g.affine_select(out=masks[:, 7, :], in_=masks[:, 7, :], compare_op=ALU.is_ge, fill=0.0, base=0,
                    pattern=[[1, P]], channel_multiplier=-1)
    g.affine_select(out=masks[:, 8, :], in_=masks[:, 8, :], compare_op=ALU.is_gt, fill=0.0, base=0,
                    pattern=[[1, P]], channel_multiplier=-1)
    g.drain()
    g.memset(c.cons[:, 2:3], 0.0).then_inc(c.sem("masks"), 1)
    for t in range(TT):
        for b in (2 * t, 2 * t + 1):
            g.wait_ge(c.sem("decay_exps"), b + 1)
            for i, cmp, ch, st in ((5, ALU.is_gt, 1, -1), (7, ALU.is_ge, -1, 1)):
                m = c.view(BA_ + (b % 2) * 4096 + 512 * i, 4, P)
                g.affine_select(out=m, in_=m, compare_op=cmp, fill=0.0, base=0, pattern=[[0, 4], [st, P]],
                                channel_multiplier=ch).then_inc(c.sem("decay_masked"), 1)
    g.wait_ge(*c.finished("st", 2 * TT - 1))
    g.dma_start(c.view(K_, DT, S), c.y_spill).then_inc(c.sem("y_back"), 16)
    g.tensor_scalar(c.view(X_, DT * S), c.view(X_, DT * S), ALPHA, None, ALU.mult).then_inc(c.sem("x_scaled"), 1)


ADA_ = U_
MOD_TILES = 6 * D // P


def modulation(c, v):
    row, product = c.view(ADA_, D), c.view(ADA_ + D, D)
    bufs = c.view(ADA_ + 2 * D, 4, D)
    v.wait_ge(c.sem("condition"), 1)
    for i in range(MOD_TILES):
        v.wait_ge(c.sem(f"ada{i % 4}"), 16 * (i // 4 + 1))
        v.tensor_tensor_reduce(out=product, in0=bufs[:, i % 4, :], in1=row, scale=1.0, scalar=0.0,
                               op0=ALU.mult, op1=ALU.add, accum_out=c.mod[:, i:i + 1]).then_inc(c.sem("ada_used"), 1)
        v.drain()
        yield
    v.wait_ge(c.sem("vectors"), 16)
    at, n = VECS["b_ada_2"]
    v.tensor_tensor(c.mod[:, :], c.mod[:, :], c.vecs[:, at:at + n], ALU.add)
    v.drain()
    v.tensor_scalar(c.mod[:, 8:24], c.mod[:, 8:24], 1.0, None, ALU.add)
    v.tensor_scalar(c.mod[:, 32:48], c.mod[:, 32:48], 1.0, None, ALU.add)
    v.drain()
    v.memset(c.cons[:, 3:4], 0.0).then_inc(c.sem("mod"), 1)


def modulation_act(c, a):
    row = c.view(ADA_, D)
    a.wait_ge(c.sem("condition_in"), 16)
    a.activation(row, row, ACT.Silu).then_inc(c.sem("condition"), 1)


def modulation_pool(c, g):
    g.dma_start(c.view(ADA_, D), c.args["c"].to_broadcast([P, D])).then_inc(c.sem("condition_in"), 16)
    for i in range(MOD_TILES):
        if i >= 4:
            g.wait_ge(c.sem("ada_used"), i - 3)
        g.dma_start(c.view(ADA_ + (2 + i % 4) * D, D), c.args["w_adaT"][i]).then_inc(c.sem(f"ada{i % 4}"), 16)


XTOK_, HTOK_ = B0, B0 + 4096
RT_ = B0 + 8192
RT_LG, RT_EXP, RT_SEL, RT_RANK, RT_TOT = 0, 144, 164, 292, 420
RT_OH1, RT_OH2, RT_OHG, RT_ING, RT_O1, RT_O2, RT_T, RT_DESC, RT_THR, RT_BLK = \
    452, 580, 708, 724, 756, 788, 820, 1332, 1340, 1348
RT_NB, RT_END, RT_POS, RT_S, RT_BE, RT_X = 1396, 1428, 1460, 1588, 1620, 1680
ROUTE = 1680 + NB * NE
GATE_S, DEST_S, BLK_S = 484, 492, 500


def route_dve(c, v):
    r = c.route

    def T(at, *shape):
        n = int(np.prod(shape))
        s = r[:, at:at + n]
        if len(shape) == 2:
            return s.rearrange("p (a b) -> p a b", a=shape[0])
        if len(shape) == 3:
            return s.rearrange("p (a b c) -> p a b c", a=shape[0], b=shape[1])
        return s

    def tt(out, a, b, op):
        v.tensor_tensor(out, a, b, op)
        v.drain()

    def red(out, a, op):
        v.tensor_reduce(out, a, AX.X, op)
        v.drain()

    def over(a, n):
        return a.unsqueeze(2).to_broadcast([P, TT, n])

    def first_max(out, values, n, top):
        desc = T(RT_DESC, 8)[:, 8 - n:8].unsqueeze(1).to_broadcast([P, TT, n])
        t, m = T(RT_T, TT, n), T(RT_S, TT)
        red(top, values, ALU.max)
        tt(t, values, over(top, n), ALU.is_equal)
        tt(t, t, desc, ALU.mult)
        red(m, t, ALU.max)
        tt(out, t, over(m, n), ALU.is_equal)

    lg = T(RT_LG, TT, 36)[:, :, 0:NG]
    le = T(RT_LG, TT, 36)[:, :, NG:]
    ex = T(RT_EXP, 20)
    gmax, m1, m2 = T(RT_S + 4, TT), T(RT_S + 8, TT), T(RT_S + 12, TT)
    ohg, ing, o1, o2 = T(RT_OHG, TT, NG), T(RT_ING, TT, EG), T(RT_O1, TT, EG), T(RT_O2, TT, EG)
    v.wait_ge(*c.put_away("rt", TT - 1))
    v.wait_ge(c.sem("counts"), 1)
    first_max(ohg, lg, NG, gmax)
    for t in range(TT):
        tt(T(RT_X, EG, NG), le[:, t, :].rearrange("p (g e) -> p e g", g=NG),
           ohg[:, t, :].unsqueeze(1).to_broadcast([P, EG, NG]), ALU.mult)
        red(ing[:, t, :], T(RT_X, EG, NG), ALU.add)
    first_max(o1, ing, EG, m1)
    v.scalar_tensor_tensor(ing, o1, SET_ASIDE, ing, ALU.mult, ALU.add)
    v.drain()
    first_max(o2, ing, EG, m2)
    tt(T(RT_EXP, TT, NG), lg, over(gmax, NG), ALU.subtract)
    v.tensor_tensor(ex[:, 16:20], m2, m1, ALU.subtract).then_inc(c.sem("route_exp"), 1)
    oh = (T(RT_OH1, TT, NG, EG), T(RT_OH2, TT, NG, EG))
    for t in range(TT):
        for k, o in enumerate((o1, o2)):
            v.tensor_tensor(oh[k][:, t], ohg[:, t, :].unsqueeze(2).to_broadcast([P, NG, EG]),
                            o[:, t, :].unsqueeze(1).to_broadcast([P, NG, EG]), ALU.mult)
    v.drain()
    v.tensor_tensor(T(RT_SEL, 128), T(RT_OH1, 128), T(RT_OH2, 128), ALU.add).then_inc(c.sem("chosen"), 1)
    v.wait_ge(c.sem("route_exps"), 1)
    gates = c.small[:, GATE_S:GATE_S + 8].rearrange("p (k t) -> p k t", k=2)
    zg, den = T(RT_S + 16, TT), T(RT_S + 20, TT)
    red(zg, T(RT_EXP, TT, NG), ALU.add)
    v.tensor_scalar(den, ex[:, 16:20], 1.0, None, ALU.add)
    v.drain()
    tt(den, den, zg, ALU.mult)
    v.reciprocal(gates[:, 0, :], den)
    v.drain()
    tt(gates[:, 1, :], gates[:, 0, :], ex[:, 16:20], ALU.mult)
    v.wait_ge(*c.put_away("total", 0))
    nb, end, x = T(RT_NB, NE), T(RT_END, NE), T(RT_X, NE, 8)
    tt(x, T(RT_TOT, NE).unsqueeze(2).to_broadcast([P, NE, 8]), T(RT_THR, 8).unsqueeze(1).to_broadcast([P, NE, 8]),
       ALU.is_gt)
    red(nb, x, ALU.add)
    v.tensor_tensor_scan(end, c.ones[:, 0:NE], nb, 0.0, ALU.mult, ALU.add)
    v.drain()
    be = T(RT_BE, NB + 1)
    x = r[0:1, RT_X:RT_X + NB * NE].rearrange("p (a b) -> p a b", a=NB)
    tt(x, end[0:1].unsqueeze(1).to_broadcast([1, NB, NE]), T(RT_BLK, NB)[0:1].unsqueeze(2).to_broadcast([1, NB, NE]),
       ALU.is_le)
    red(be[0:1, 0:NB], x, ALU.add)
    v.tensor_scalar(be[0:1, 0:NB], be[0:1, 0:NB], float(NE - 1), None, ALU.min)
    v.tensor_copy(be[0:1, NB:NB + 1], end[0:1, NE - 1:NE])
    v.drain()
    v.tensor_copy(c.small[0:1, BLK_S:BLK_S + NB + 1].bitcast(I32), be[0:1]).then_inc(c.sem("blocks"), 1)
    tt(nb, end, nb, ALU.subtract)
    v.tensor_scalar(nb, nb, float(SLOTS), None, ALU.mult)
    v.drain()
    pos = T(RT_POS, TT, NE)
    tt(pos, T(RT_RANK, TT, NE), nb.unsqueeze(1).to_broadcast([P, TT, NE]), ALU.add)
    dest = T(RT_S + 24, 8)
    for k in range(2):
        tt(T(RT_X, TT, NE), T((RT_OH1, RT_OH2)[k], TT, NE), pos, ALU.mult)
        red(dest[:, 4 * k:4 * k + 4], T(RT_X, TT, NE), ALU.add)
    v.tensor_copy(c.small[:, DEST_S:DEST_S + 8].bitcast(I32), dest).then_inc(c.sem("destinations"), 1)
    xtok = c.view(XTOK_, TT, D)
    for i in range(2 * TT):
        v.wait_ge(*c.finished("xt", i))
        bank = c.bank("xt", i)
        v.tensor_scalar(xtok[:, i // 2, 512 * (i % 2):512 * (i % 2) + 512], bank, ALPHA, None, ALU.mult) \
            .then_inc(c.emptied("dve", "xt", i), 1)


def route_pool(c, g):
    r = c.route
    g.wait_ge(*c.put_away("wo2", DT - 1))
    g.iota(r[:, RT_DESC:RT_DESC + 8], pattern=[[-1, 8]], base=8, channel_multiplier=0, allow_small_or_imprecise_dtypes=True)
    g.iota(r[:, RT_THR:RT_THR + 8], pattern=[[SLOTS, 8]], base=0, channel_multiplier=0, allow_small_or_imprecise_dtypes=True)
    g.iota(r[:, RT_BLK:RT_BLK + NB], pattern=[[1, NB]], base=0, channel_multiplier=0,
           allow_small_or_imprecise_dtypes=True).then_inc(c.sem("counts"), 1)
    g.wait_ge(*c.put_away("ht", 2 * TT - 1))
    g.wait_ge(c.sem("destinations"), 1)
    g.wait_ge(c.sem("zeroed"), 32)
    htok = c.view(HTOK_, TT, D)
    for k in range(2):
        for t in range(TT):
            i = DEST_S + 4 * k + t
            g.indirect_dma_start(
                out=c.xs_rows, out_offset=bass.IndirectOffsetOnAxis(ap=c.small[:, i:i + 1].bitcast(U32), axis=0),
                in_=htok[:, t, :], in_offset=None).then_inc(c.sem("scattered"), 16)


SETS = 3
M0 = B0 + 16384
XS_ = M0
XST_ = XS_ + SETS * D
HB_ = XST_ + SETS * 512
SG_ = HB_ + SETS * EF
HT_ = SG_ + SETS * EF
YO_ = HT_ + SETS * 256
assert YO_ + D <= ARENA
EXPERT_PLACES = (("ring", 0), ("ring", 1), ("ring", 2), ("ring", 3), ("arena", 0), ("arena", 4096),
                 ("arena", B0 + 4096), ("arena", B0 + 8192), ("arena", B0 + 12288))


def expert_weights(c, j):
    out = []
    for where, at in EXPERT_PLACES[3 * j:3 * j + 3]:
        out.append(c.ring[:, at, :] if where == "ring" else c.view(at, CHUNK * P))
    return (out[0].rearrange("p (k n) -> p k n", k=8), out[1].rearrange("p (k n) -> p k n", k=8),
            out[2].rearrange("p (k n) -> p k n", k=4))


def over_blocks(c, engine, body):
    engine.wait_ge(c.sem("blocks"), 1)
    used = engine.value_load(c.small[0:1, BLK_S + NB:BLK_S + NB + 1].bitcast(I32), min_val=0, max_val=NB)
    with engine.Fori(0, NB // SETS) as i:
        for j in range(SETS):
            with engine.If(i * SETS + j < used):
                body(i, i * SETS + j, j)
    return used


def experts_sp(c, sp):
    sp.wait_ge(*c.finished("xt", 2 * TT - 1))
    sp.wait_ge(c.sem("scattered"), 16 * 2 * TT)
    sp.wait_ge(c.sem("destinations"), 1)

    def body(i, n, j):
        e = sp.value_load(c.small[0:1, bass.ds(n + BLK_S, 1)].bitcast(I32), min_val=0, max_val=NE - 1)
        sp.wait_ge(c.sem(f"weights_used{j}"), i + 1)
        for part, dst in enumerate(expert_weights(c, j)):
            sp.dma_start(dst.rearrange("p k n -> p (k n)"),
                         c.args["experts"][bass.ds(e, 1), part].rearrange("a p n -> (a p) n")) \
                .then_inc(c.sem(f"expert{part}_{j}"), 16)
            if part == 0:
                sp.dma_start(c.view(XS_ + j * D, D)[0:SLOTS], c.xs_blocks[bass.ds(n, 1)].rearrange("a p n -> (a p) n")) \
                    .then_inc(c.sem(f"rows{j}"), 16)
    over_blocks(c, sp, body)


def experts_pe(c, pe):
    pe.wait_ge(*c.put_away("xt", 2 * TT - 1))
    pe.wait_ge(*c.put_away("total", 0))

    def body(i, n, j):
        xs, xsT = c.view(XS_ + j * D, D), c.view(XST_ + j * 512, 8, SLOTS)
        hb, hT = c.view(HB_ + j * EF, EF), c.view(HT_ + j * 256, 4, SLOTS)
        wg, wu, wd = expert_weights(c, j)
        turned = c.ps[:, j, :]
        pe.wait_ge(c.sem(f"rows{j}"), 16 * (i + 1))
        pe.sem_inc(c.sem("passed"), 1)
        for k in range(DT):
            m = pe.transpose(turned[:, k * SLOTS:(k + 1) * SLOTS], xs[0:SLOTS, k * P:(k + 1) * P],
                             c.ident[0:SLOTS, 0:SLOTS])
        m.then_inc(c.sem(f"turned{j}"), 1)
        pe.wait_ge(c.sem(f"expert0_{j}"), 16 * (i + 1))
        pe.wait_ge(c.sem(f"turned_copied{j}"), i + 1)
        pe.sem_inc(c.sem("passed"), 1)
        for k in range(DT):
            m = pe.matmul(c.ps[0:SLOTS, 3, :], xsT[:, k, :], wg[:, k, :], start=k == 0, stop=k == DT - 1)
        m.then_inc(c.sem(f"gate_product{j}"), 1)
        pe.wait_ge(c.sem(f"expert1_{j}"), 16 * (i + 1))
        pe.sem_inc(c.sem("passed"), 1)
        for k in range(DT):
            m = pe.matmul(c.ps[0:SLOTS, 4, :], xsT[:, k, :], wu[:, k, :], start=k == 0, stop=k == DT - 1)
        m.then_inc(c.sem(f"up_product{j}"), 1)
        pe.wait_ge(c.sem(f"hidden{j}"), i + 1)
        pe.sem_inc(c.sem("passed"), 1)
        for f in range(EF // P):
            m = pe.transpose(turned[:, f * SLOTS:(f + 1) * SLOTS], hb[0:SLOTS, f * P:(f + 1) * P],
                             c.ident[0:SLOTS, 0:SLOTS])
        m.then_inc(c.sem(f"hidden_turned{j}"), 1)
        pe.wait_ge(c.sem(f"expert2_{j}"), 16 * (i + 1))
        pe.wait_ge(c.sem(f"hidden_copied{j}"), i + 1)
        pe.wait_ge(c.sem("shared_read"), n + 1)
        pe.sem_inc(c.sem("passed"), 1)
        for half in range(2):
            for k in range(EF // P):
                m = pe.matmul(c.ps[0:SLOTS, 6 + half, :], hT[:, k, :], wd[:, k, 512 * half:512 * half + 512],
                              start=k == 0, stop=k == EF // P - 1)
        m.then_inc(c.sem(f"weights_used{j}"), 1)
    return over_blocks(c, pe, body)


def experts_act(c, a):
    def body(i, n, j):
        a.wait_ge(c.sem(f"turned{j}"), i + 1)
        a.activation(c.view(XST_ + j * 512, 512), c.ps[:, j, :], ACT.Copy).then_inc(c.sem(f"turned_copied{j}"), 1)
        a.wait_ge(c.sem(f"gate_product{j}"), i + 1)
        a.activation(c.view(SG_ + j * EF, EF)[0:SLOTS], c.ps[0:SLOTS, 3, :], ACT.Silu).then_inc(c.sem(f"silu{j}"), 1)
    over_blocks(c, a, body)


def experts_dve(c, v):
    def body(i, n, j):
        v.wait_ge(c.sem(f"silu{j}"), i + 1)
        v.wait_ge(c.sem(f"up_product{j}"), i + 1)
        v.tensor_tensor(c.view(HB_ + j * EF, EF)[0:SLOTS], c.view(SG_ + j * EF, EF)[0:SLOTS], c.ps[0:SLOTS, 4, :],
                        ALU.mult).then_inc(c.sem(f"hidden{j}"), 1)
        v.wait_ge(c.sem(f"hidden_turned{j}"), i + 1)
        v.tensor_copy(c.view(HT_ + j * 256, 256), c.ps[:, j, 0:256]).then_inc(c.sem(f"hidden_copied{j}"), 1)
        v.wait_ge(c.sem(f"weights_used{j}"), i + 2)
        v.wait_ge(c.sem("output_free"), n + 1)
        v.tensor_copy(c.view(YO_, D)[0:SLOTS], c.ps[0:SLOTS, 6:8, :].rearrange("p a b -> p (a b)")) \
            .then_inc(c.sem("shared_read"), 1)
    over_blocks(c, v, body)


def experts_pool(c, g):
    def body(i, n, j):
        g.wait_ge(c.sem("shared_read"), n + 2)
        g.dma_start(c.y_blocks[bass.ds(n, 1)].rearrange("a p n -> (a p) n"), c.view(YO_, D)[0:SLOTS]) \
            .then_inc(c.sem("stored_rows"), 16)
        g.wait_ge(c.sem("stored_rows"), 16 * n + 16)
        g.sem_inc(c.sem("output_free"), 1)
    for j in range(SETS):
        g.sem_inc(c.sem(f"weights_used{j}"), 1)
    g.sem_inc(c.sem("shared_read"), 1)
    g.sem_inc(c.sem("output_free"), 1)
    return over_blocks(c, g, body)


GROW_, LNG_, LNB_ = B0 + 4096, B0 + 5120, B0 + 6144
Z_ = B0 + 8192
FIN_S = 556


def final_pe(c, pe, used):
    pe.wait_ge(c.sem("shared_read"), used + 1)
    for k in range(DT):
        m = pe.matmul(c.ps[:, 6 + k // 4, k % 4 * P:(k % 4 + 1) * P], c.mod[:, 40 + k:41 + k].to_broadcast([P, P]),
                      c.ident[:, :], start=True, stop=True)
    m.then_inc(c.sem("gate_row"), 1)


def final_act(c, a):
    a.wait_ge(c.sem("gate_row"), 1)
    a.activation(c.view(GROW_, D), c.ps[:, 6:8, :].rearrange("p a b -> p (a b)"), ACT.Copy) \
        .then_inc(c.sem("gate_row_copied"), 1)
    fin = c.small[:, FIN_S:FIN_S + 20]
    for t in range(TT):
        z = c.view(Z_ + t * D, D)
        a.wait_ge(c.sem("mean_known"), t + 1)
        a.activation(z, z, ACT.Identity, bias=fin[:, t:t + 1]).then_inc(c.sem("last_centred"), 1)
        a.drain()
        a.activation(c.view(B0 + 12288 + t % 2 * D, D), z, ACT.Square, accum_out=fin[:, 4 + t:5 + t])
        a.drain()
        a.activation(fin[:, 8 + t:9 + t], fin[:, 4 + t:5 + t], ACT.Sqrt, bias=c.cons[:, 1:2], scale=1.0 / D) \
            .then_inc(c.sem("last_root"), 1)


def final_dve(c, v):
    gates = c.small[:, GATE_S:GATE_S + 8].rearrange("p (k t) -> p k t", k=2)
    fin = c.small[:, FIN_S:FIN_S + 20]
    xtok = c.view(XTOK_, TT, D)
    row, lng, lnb = c.view(GROW_, D), c.view(LNG_, D), c.view(LNB_, D)
    v.wait_ge(c.sem("gate_row_copied"), 1)
    for t in range(TT):
        z = c.view(Z_ + t * D, D)
        v.wait_ge(c.sem(f"gathered{t}"), 16)
        v.tensor_scalar(z, c.view(t * D, D), gates[:, 0, t:t + 1], None, ALU.mult)
        v.drain()
        v.wait_ge(c.sem(f"gathered{4 + t}"), 16)
        v.scalar_tensor_tensor(z, c.view((4 + t) * D, D), gates[:, 1, t:t + 1], z, ALU.mult, ALU.add)
        v.drain()
        v.tensor_tensor(z, z, row, ALU.mult)
        v.drain()
        v.scalar_tensor_tensor(z, z, 1.0, xtok[:, t, :], ALU.mult, ALU.add, accum_out=fin[:, 12 + t:13 + t])
        v.drain()
        v.tensor_scalar(fin[:, t:t + 1], fin[:, 12 + t:13 + t], -1.0 / D, None, ALU.mult).then_inc(c.sem("mean_known"), 1)
    v.wait_ge(c.sem("norm_rows"), 32)
    for t in range(TT):
        z = c.view(Z_ + t * D, D)
        v.wait_ge(c.sem("last_root"), t + 1)
        v.reciprocal(fin[:, 16 + t:17 + t], fin[:, 8 + t:9 + t])
        v.drain()
        v.scalar_tensor_tensor(z, z, fin[:, 16 + t:17 + t], lng, ALU.mult, ALU.mult)
        v.drain()
        v.tensor_tensor(z, z, lnb, ALU.add).then_inc(c.sem("finished"), 1)


def final_pool(c, g, used):
    g.wait_ge(c.sem("output_free"), used + 1)
    g.sem_inc(c.sem("all_stored"), 1)
    for k in range(2):
        for t in range(TT):
            i = DEST_S + 4 * k + t
            g.indirect_dma_start(
                out=c.view((4 * k + t) * D, D), out_offset=None, in_=c.y_rows,
                in_offset=bass.IndirectOffsetOnAxis(ap=c.small[:, i:i + 1].bitcast(U32), axis=0)) \
                .then_inc(c.sem(f"gathered{4 * k + t}"), 16)


def final_sp(c, sp):
    sp.wait_ge(c.sem("gate_row"), 1)
    for at, name in ((LNG_, "ln_g_row"), (LNB_, "ln_b_row")):
        sp.dma_start(c.view(at, D), c.args[name].to_broadcast([P, D])).then_inc(c.sem("norm_rows"), 16)
    for t in range(TT):
        sp.wait_ge(c.sem("finished"), t + 1)
        sp.dma_start(c.args["out"][t * P:(t + 1) * P, :], c.view(Z_ + t * D, D)).then_inc(c.sem("stored"), 16)
    sp.wait_ge(c.sem("stored"), 16 * TT)


def constants_pool(c, g):
    g.memset(c.cons[:, 0:1], EPS)
    g.memset(c.view(U_, CT * (S + CK - 1)), 0.0).then_inc(c.sem("pads"), 1)
    g.memset(c.ones[:, :], 1.0).then_inc(c.sem("constants"), 1)
    g.drain()
    g.affine_select(out=c.ident[:, :], in_=c.ones[:, :], compare_op=ALU.is_equal, fill=0.0, base=0,
                    pattern=[[-1, P]], channel_multiplier=1).then_inc(c.sem("constants"), 1)


def program(nc, plan, args):
    with ExitStack() as ctx:
        c = Core(nc, ctx, plan, args)
        block = ctx.enter_context(nc.Block())

        @block.tensor
        def _(pe):
            first_pe(c, pe)
            second_pe(c, pe)
            used = experts_pe(c, pe)
            final_pe(c, pe, used)

        @block.scalar
        def _(act):
            first_act(c, act)
            second_act(c, act)
            experts_act(c, act)
            final_act(c, act)

        @block.vector
        def _(dve):
            first_dve(c, dve)
            dve.drain()
            second_dve(c, dve)
            route_dve(c, dve)
            experts_dve(c, dve)
            final_dve(c, dve)

        @block.gpsimd
        def _(pool):
            constants_pool(c, pool)
            first_pool(c, pool)
            pool.wait_ge(*c.put_away("mo", DT - 1))
            modulation_pool(c, pool)
            second_pool(c, pool)
            route_pool(c, pool)
            used = experts_pool(c, pool)
            final_pool(c, pool, used)

        @block.sync
        def _(sp):
            x = c.view(X_, DT, S)
            for k in range(2):
                sp.dma_start(x[:, 4 * k:4 * k + 4, :], args["xT"][:, 4 * k:4 * k + 4, :]).then_inc(c.sem(f"x{k}"), 16)
            sp.dma_start(c.vecs[:, :], args["vecs"]).then_inc(c.sem("vectors"), 16)
            sp.dma_start(c.view(TMP_ + 2 * S, S).bitcast(I32), args["positions"].to_broadcast([P, S])) \
                .then_inc(c.sem("positions"), 16)
            for at, name in ((NALOG_S, "a_log"), (DTB_S, "dt_bias")):
                sp.dma_start(c.small[:, at:at + 32], args[name].to_broadcast([P, 32])) \
                    .then_inc(c.sem("decay_params"), 16)
            load_weights(c, sp)
            experts_sp(c, sp)
            final_sp(c, sp)


def kernel(**inputs):
    import concourse.bacc as _bacc
    from concourse.bass_utils import run_bass_kernel_spmd as _run
    inputs = {k: np.asarray(v) for k, v in inputs.items()}
    inputs["route"] = np.concatenate([inputs["w_route_grp_2"][0], inputs["w_route_exp_2"][0]], axis=1)
    plan = make_plan()
    arrays = {
        "xT": inputs["x"][0].T.reshape(DT, P, S).transpose(1, 0, 2),
        "vecs": vec_array(inputs),
        "stream": stream_array(inputs, plan),
        "positions": inputs["positions"],
        "c": inputs["c_2"],
        "w_adaT": inputs["w_ada_2"][0].T.reshape(MOD_TILES, P, D),
        "a_log": np.tile(inputs["a_log_2"], (1, TT)),
        "dt_bias": np.tile(inputs["dt_bias_2"], (1, TT)),
        "zeros": np.zeros((1, SLOTS, D), np.float32),
        "experts": experts_array(inputs),
        "ln_g_row": inputs["ln_g_2"][:, 1],
        "ln_b_row": inputs["ln_b_2"][:, 1],
    }
    arrays = {k: np.ascontiguousarray(a) for k, a in arrays.items()}
    nc = _bacc.Bacc("TRN2", target_bir_lowering=False, num_devices=1)
    args = {k: nc.dram_tensor("in_" + k, a.shape, mybir.dt.from_np(a.dtype), kind="ExternalInput").ap()
            for k, a in arrays.items()}
    args["out"] = nc.dram_tensor("out_0", (S, D), F32, kind="ExternalOutput").ap()
    program(nc, plan, args)
    r = _run(nc, [{"in_" + k: a for k, a in arrays.items()}], core_ids=[0])
    return r.results[0]["out_0"].reshape(1, S, D)
```
